# Optimizing a Trainium2 kernel written in Bass

```python
import math
import jax, jax.numpy as jnp
from jax import lax
import numpy as np

D_MODEL = 1024
BATCH = 1
SEQ = 512
DEPTH = 2

CTX_LEN = 256
GRID_W = 64
EPS = 1e-6
ROPE_BASE = 10000.0
Q_BLOCK = 128
f32 = jnp.float32

H_A = 4
DH_A = 64
DV_A = 2 * DH_A
A_W = H_A * DV_A
H_B = 4
DH_B = 128
B_W = H_B * DH_B
GDN_CHUNK = 64
CONV_K = 5
H_C = 8
DH_C = 128
WIN_R = 8
WIN_C = 16
MIX_ODD = H_C * DH_C

MIX_EVEN = A_W + B_W
EVEN_IN = 3 * A_W + 4 * B_W + 4 * H_B
EVEN_CUTS = [A_W, 2 * A_W, 3 * A_W, 3 * A_W + 3 * B_W, 3 * A_W + 4 * B_W]
FF_HIDDEN = ((8 * D_MODEL // 3 + 255) // 256) * 256
N_EVEN = (DEPTH + 1) // 2
N_ODD = DEPTH // 2


def rms_norm(x, gain):
    xf = x.astype(f32)
    y = xf * lax.rsqrt(jnp.mean(xf * xf, axis=-1, keepdims=True) + EPS)
    return (y * gain.astype(f32)).astype(x.dtype)

def l2_norm(x):
    return x * lax.rsqrt(jnp.sum(x * x, axis=-1, keepdims=True) + EPS)

def heads(t, n):
    b, l, _ = t.shape
    return t.reshape(b, l, n, -1).transpose(0, 2, 1, 3)

def merge_heads(t):
    b, h, l, d = t.shape
    return t.transpose(0, 2, 1, 3).reshape(b, l, h * d)

def axial_rope(l, dim):
    n_freq = dim // 4
    inv = ROPE_BASE ** (-jnp.arange(n_freq, dtype=f32) / n_freq)
    t = jnp.arange(l)
    row = (t // GRID_W).astype(f32)
    col = (t % GRID_W).astype(f32)
    ang = jnp.concatenate([row[:, None] * inv, col[:, None] * inv], axis=-1)
    return jnp.cos(ang), jnp.sin(ang)

def apply_rope(x, cos, sin):
    xf = x.astype(f32).reshape(*x.shape[:-1], x.shape[-1] // 2, 2)
    x0, x1 = xf[..., 0], xf[..., 1]
    out = jnp.stack([x0 * cos - x1 * sin, x0 * sin + x1 * cos], axis=-1)
    return out.reshape(x.shape).astype(x.dtype)

def softmax_attention(q, k, v):
    s = jnp.einsum('bhqd,bhkd->bhqk', q, k).astype(f32) * (q.shape[-1] ** -0.5)
    return jnp.einsum('bhqk,bhkd->bhqd', jax.nn.softmax(s, axis=-1).astype(v.dtype), v)

def over_query_blocks(fn, qs):
    b, h, l, _ = qs[0].shape
    nb = l // Q_BLOCK
    blocked = tuple(jnp.moveaxis(t.reshape(b, h, nb, Q_BLOCK, t.shape[-1]), 2, 0) for t in qs)
    out = lax.map(lambda qq: fn(*qq), blocked)
    return jnp.moveaxis(out, 0, 2).reshape(b, h, l, out.shape[-1])

def diff_core(q1, q2, k1, k2, v, lam):
    scale = DH_A ** -0.5
    p1 = jax.nn.softmax(jnp.einsum('bhqd,bhkd->bhqk', q1, k1).astype(f32) * scale, axis=-1)
    p2 = jax.nn.softmax(jnp.einsum('bhqd,bhkd->bhqk', q2, k2).astype(f32) * scale, axis=-1)
    return jnp.einsum('bhqk,bhkd->bhqd', (p1 - lam * p2).astype(v.dtype), v)

def diff_attention(q, k, v, qc, kc, vc, qk_gain, lam_vec, subln, lam_init, cos, sin, ctx_out):
    lv = lam_vec.astype(f32)
    lam = jnp.exp(jnp.sum(lv[0] * lv[1])) - jnp.exp(jnp.sum(lv[2] * lv[3])) + lam_init

    def split_maps(t, gain, rope):
        t = heads(t, H_A)
        b, h, l, _ = t.shape
        t = rms_norm(t.reshape(b, h, l, 2, DH_A), gain)
        t1, t2 = t[..., 0, :], t[..., 1, :]
        if rope:
            t1, t2 = apply_rope(t1, cos, sin), apply_rope(t2, cos, sin)
        return t1, t2

    q1, q2 = split_maps(q, qk_gain[0], True)
    k1, k2 = split_maps(k, qk_gain[1], True)
    k1c, k2c = split_maps(kc, qk_gain[1], False)
    vh, vch = heads(v, H_A), heads(vc, H_A)
    k1a = jnp.concatenate([k1c, k1], axis=2)
    k2a = jnp.concatenate([k2c, k2], axis=2)
    va = jnp.concatenate([vch, vh], axis=2)
    o = over_query_blocks(lambda a, b_: diff_core(a, b_, k1a, k2a, va, lam), (q1, q2))

    def post(t):
        return merge_heads(rms_norm(t, subln) * (1.0 - lam_init))

    oc = None
    if ctx_out:
        q1c, q2c = split_maps(qc, qk_gain[0], False)
        oc = post(diff_core(q1c, q2c, k1c, k2c, vch, lam))
    return post(o), oc

def short_conv(t, w):
    c = t.shape[-1]
    y = lax.conv_general_dilated(t, w[:, None, :].astype(t.dtype), window_strides=(1,),
                                 padding=[(CONV_K // 2, CONV_K // 2)],
                                 dimension_numbers=('NWC', 'WIO', 'NWC'), feature_group_count=c)
    return jax.nn.silu(y)

def gdn_inputs(qkv, gates, conv_w, a_log, dt_bias):
    y = short_conv(qkv, conv_w).astype(f32)
    q, k, v = jnp.split(y, 3, axis=-1)
    q = l2_norm(heads(q, H_B)) * (DH_B ** -0.5)
    k = l2_norm(heads(k, H_B))
    v = heads(v, H_B)
    b, l, _ = gates.shape
    g = gates.astype(f32).transpose(0, 2, 1)
    beta = jax.nn.sigmoid(g[:, :2 * H_B]).reshape(b, 2, H_B, l)
    a = g[:, 2 * H_B:].reshape(b, 2, H_B, l)
    log_alpha = -jnp.exp(a_log.astype(f32))[None, :, :, None] * jax.nn.softplus(a + dt_bias.astype(f32)[None, :, :, None])
    return q, k, v, log_alpha, beta

def gated_delta_chunked(q, k, v, log_a, beta, s0):
    b, h, l, dk = q.shape
    dv = v.shape[-1]
    n = l // GDN_CHUNK
    rs = lambda t: t.reshape(b, h, n, GDN_CHUNK, *t.shape[3:])
    q, k, v, log_a, beta = rs(q), rs(k), rs(v), rs(log_a), rs(beta)
    g = jnp.cumsum(log_a, axis=-1)
    idx = jnp.arange(GDN_CHUNK)
    causal = idx[:, None] >= idx[None, :]
    strict = idx[:, None] > idx[None, :]
    decay = jnp.exp(jnp.where(causal, g[..., :, None] - g[..., None, :], -jnp.inf))
    kk = jnp.einsum('bhncd,bhnsd->bhncs', k, k)
    lmat = jnp.where(strict, beta[..., :, None] * decay * kk, 0.0)
    rhs = jnp.concatenate([beta[..., None] * v, (beta * jnp.exp(g))[..., None] * k], axis=-1)
    sol = lax.linalg.triangular_solve(jnp.eye(GDN_CHUNK, dtype=f32) + lmat, rhs,
                                      left_side=True, lower=True, unit_diagonal=True)
    u0, w = sol[..., :dv], sol[..., dv:]
    aqk = jnp.einsum('bhncd,bhnsd->bhncs', q, k) * decay
    qg = q * jnp.exp(g)[..., None]
    kg = k * jnp.exp(g[..., -1:] - g)[..., None]
    gl = jnp.exp(g[..., -1])

    def step(s, inp):
        u0_c, w_c, aqk_c, qg_c, kg_c, gl_c = inp
        u = u0_c - w_c @ s
        o = qg_c @ s + aqk_c @ u
        s = gl_c[..., None, None] * s + jnp.swapaxes(kg_c, -1, -2) @ u
        return s, o

    xs = tuple(jnp.moveaxis(t, 2, 0) for t in (u0, w, aqk, qg, kg, gl))
    s_fin, o = lax.scan(step, s0, xs)
    return jnp.moveaxis(o, 0, 2).reshape(b, h, l, dv), s_fin

def bidirectional_delta(lat, ctx):
    q, k, v, la, be = lat
    qc, kc, vc, lac, bec = ctx
    s0 = jnp.zeros((q.shape[0], H_B, DH_B, DH_B), f32)
    fl = lambda t: jnp.flip(t, axis=2)
    oc_f, s_f = gated_delta_chunked(qc, kc, vc, lac[:, 0], bec[:, 0], s0)
    oc_b, s_b = gated_delta_chunked(fl(qc), fl(kc), fl(vc), fl(lac[:, 1]), fl(bec[:, 1]), s0)
    o_f, _ = gated_delta_chunked(q, k, v, la[:, 0], be[:, 0], s_f)
    o_b, _ = gated_delta_chunked(fl(q), fl(k), fl(v), fl(la[:, 1]), fl(be[:, 1]), s_b)
    return o_f + fl(o_b), oc_f + fl(oc_b)

def gated_deltanet(qkv, gate, gates, qkv_c, gate_c, gates_c, conv_w, a_log, dt_bias, gain, ctx_out):
    lat = gdn_inputs(qkv, gates, conv_w, a_log, dt_bias)
    ctxi = gdn_inputs(qkv_c, gates_c, conv_w, a_log, dt_bias)
    o_lat, o_ctx = bidirectional_delta(lat, ctxi)

    def post(o, gg):
        b, l, _ = gg.shape
        o = rms_norm(o.transpose(0, 2, 1, 3), gain) * jax.nn.silu(gg.astype(f32).reshape(b, l, H_B, DH_B))
        return o.reshape(b, l, B_W).astype(gg.dtype)

    return post(o_lat, gate), (post(o_ctx, gate_c) if ctx_out else None)

def even_mixer(h, hc, w_in, w_out, qk_gain, lam_vec, subln, lam_init, conv_w, a_log, dt_bias,
               gdn_gain, cos, sin, ctx_out):
    qa, ka, va, qkv_b, g_b, gates_b = jnp.split(h @ w_in, EVEN_CUTS, axis=-1)
    qac, kac, vac, qkv_bc, g_bc, gates_bc = jnp.split(hc @ w_in, EVEN_CUTS, axis=-1)
    a_lat, a_ctx = diff_attention(qa, ka, va, qac, kac, vac, qk_gain, lam_vec, subln, lam_init,
                                  cos, sin, ctx_out)
    b_lat, b_ctx = gated_deltanet(qkv_b, g_b, gates_b, qkv_bc, g_bc, gates_bc, conv_w, a_log,
                                  dt_bias, gdn_gain, ctx_out)
    out = jnp.concatenate([a_lat, b_lat], axis=-1) @ w_out
    out_c = jnp.concatenate([a_ctx, b_ctx], axis=-1) @ w_out if ctx_out else None
    return out, out_c

def neighbourhood_attention(q, k, v, k_ctx, v_ctx, rpb):
    b, h, l, d = q.shape
    rows = l // GRID_W
    wr = min(WIN_R, rows)
    scale = d ** -0.5
    grid = lambda t: t.reshape(b, h, rows, GRID_W, d)
    qg, kg, vg = grid(q), grid(k), grid(v)
    cols = np.arange(GRID_W)
    c_start = np.clip(cols - WIN_C // 2, 0, GRID_W - WIN_C)
    col_mask = (cols[None, :] >= c_start[:, None]) & (cols[None, :] < c_start[:, None] + WIN_C)
    dc_idx = np.clip(cols[None, :] - cols[:, None] + WIN_C - 1, 0, 2 * WIN_C - 2)
    rpb_c = rpb[:, :, dc_idx]

    def row_block(r):
        r_start = jnp.clip(r - wr // 2, 0, rows - wr)
        q_r = lax.dynamic_index_in_dim(qg, r, axis=2, keepdims=False)
        k_b = lax.dynamic_slice_in_dim(kg, r_start, wr, axis=2)
        v_b = lax.dynamic_slice_in_dim(vg, r_start, wr, axis=2)
        dr_idx = r_start + jnp.arange(wr) - r + WIN_R - 1
        bias = jnp.take(rpb_c, dr_idx, axis=1).transpose(0, 2, 1, 3)
        s_lat = jnp.einsum('bhqd,bhrkd->bhqrk', q_r, k_b).astype(f32) * scale + bias.astype(f32)
        s_lat = jnp.where(col_mask[:, None, :], s_lat, -jnp.inf).reshape(b, h, GRID_W, wr * GRID_W)
        s_ctx = jnp.einsum('bhqd,bhkd->bhqk', q_r, k_ctx).astype(f32) * scale
        p = jax.nn.softmax(jnp.concatenate([s_lat, s_ctx], axis=-1), axis=-1).astype(v.dtype)
        p_lat = p[..., :wr * GRID_W].reshape(b, h, GRID_W, wr, GRID_W)
        return (jnp.einsum('bhqrk,bhrkd->bhqd', p_lat, v_b)
                + jnp.einsum('bhqk,bhkd->bhqd', p[..., wr * GRID_W:], v_ctx))

    out = lax.map(row_block, jnp.arange(rows))
    return jnp.moveaxis(out, 0, 2).reshape(b, h, l, d)

def odd_mixer(h, hc, w_in, w_out, qk_gain, rpb, ctx_out):
    q, k, v = jnp.split(h @ w_in, 3, axis=-1)
    kc, vc = jnp.split(hc @ w_in[:, MIX_ODD:], 2, axis=-1)
    q, k, v = rms_norm(heads(q, H_C), qk_gain[0]), rms_norm(heads(k, H_C), qk_gain[1]), heads(v, H_C)
    kc, vc = rms_norm(heads(kc, H_C), qk_gain[1]), heads(vc, H_C)
    out = merge_heads(neighbourhood_attention(q, k, v, kc, vc, rpb)) @ w_out
    out_c = None
    if ctx_out:
        qc = rms_norm(heads(hc @ w_in[:, :MIX_ODD], H_C), qk_gain[0])
        out_c = merge_heads(softmax_attention(qc, kc, vc)) @ w_out
    return out, out_c

def swiglu(h, w_in, w_out):
    gt, up = jnp.split(h @ w_in, 2, axis=-1)
    return (jax.nn.silu(gt) * up) @ w_out

def first_inputs(seed: int = 0) -> dict:
    key = jax.random.key(seed)
    ks = jax.random.split(key, 24)
    d = D_MODEL
    nrm = lambda k, shape, s: jax.random.normal(k, shape, f32) * s
    dt = jnp.exp(jax.random.uniform(ks[17], (N_EVEN, 2, H_B), f32, math.log(1e-3), math.log(1e-1)))
    return {
        "x": nrm(ks[0], (BATCH, SEQ, d), 1.0),
        "c": nrm(ks[1], (BATCH, d), 1.0),
        "ctx": nrm(ks[2], (BATCH, CTX_LEN, d), 1.0),
        "c_ctx": nrm(ks[3], (d,), 1.0),
        "ada_w": nrm(ks[4], (DEPTH, d, 6 * d), 0.5 * d ** -0.5),
        "ada_b": nrm(ks[5], (DEPTH, 6 * d), 0.01),
        "norm_mix": 1.0 + nrm(ks[6], (DEPTH, d), 0.02),
        "norm_ffn": 1.0 + nrm(ks[7], (DEPTH, d), 0.02),
        "ffn_w_in": nrm(ks[8], (DEPTH, d, 2 * FF_HIDDEN), d ** -0.5),
        "ffn_w_out": nrm(ks[9], (DEPTH, FF_HIDDEN, d), FF_HIDDEN ** -0.5),
        "even_w_in": nrm(ks[10], (N_EVEN, d, EVEN_IN), d ** -0.5),
        "even_w_out": nrm(ks[11], (N_EVEN, MIX_EVEN, d), MIX_EVEN ** -0.5),
        "diff_qk_gain": 1.0 + nrm(ks[12], (N_EVEN, 2, DH_A), 0.02),
        "diff_lambda": nrm(ks[13], (N_EVEN, 4, DH_A), 0.1),
        "diff_subln": 1.0 + nrm(ks[14], (N_EVEN, DV_A), 0.02),
        "gdn_conv": nrm(ks[15], (N_EVEN, CONV_K, 3 * B_W), CONV_K ** -0.5),
        "gdn_a_log": jnp.log(jax.random.uniform(ks[16], (N_EVEN, 2, H_B), f32, 1.0, 16.0)),
        "gdn_dt_bias": dt + jnp.log(-jnp.expm1(-dt)),
        "gdn_norm": 1.0 + nrm(ks[18], (N_EVEN, DH_B), 0.02),
        "odd_w_in": nrm(ks[19], (N_ODD, d, 3 * MIX_ODD), d ** -0.5),
        "odd_w_out": nrm(ks[20], (N_ODD, MIX_ODD, d), MIX_ODD ** -0.5),
        "na_qk_gain": 1.0 + nrm(ks[21], (N_ODD, 2, DH_C), 0.02),
        "na_rpb": nrm(ks[22], (N_ODD, H_C, 2 * WIN_R - 1, 2 * WIN_C - 1), 0.02),
    }

def first_block(x, c, ctx, c_ctx, ada_w, ada_b, norm_mix, norm_ffn, ffn_w_in, ffn_w_out,
              even_w_in, even_w_out, diff_qk_gain, diff_lambda, diff_subln, gdn_conv, gdn_a_log,
              gdn_dt_bias, gdn_norm, odd_w_in, odd_w_out, na_qk_gain, na_rpb):
    cos, sin = axial_rope(x.shape[1], DH_A)
    silu_c = jax.nn.silu(c)
    silu_cc = jax.nn.silu(c_ctx)
    for l in range(DEPTH):
        ctx_out = l < DEPTH - 1
        m = silu_c @ ada_w[l] + ada_b[l]
        mc = silu_cc @ ada_w[l] + ada_b[l]
        sh_m, sc_m, g_m, sh_f, sc_f, g_f = [t[:, None, :] for t in jnp.split(m, 6, axis=-1)]
        csh_m, csc_m, cg_m, csh_f, csc_f, cg_f = jnp.split(mc, 6)
        h = rms_norm(x, norm_mix[l]) * (1.0 + sc_m) + sh_m
        hc = rms_norm(ctx, norm_mix[l]) * (1.0 + csc_m) + csh_m
        if l % 2 == 0:
            e = l // 2
            lam_init = 0.8 - 0.6 * math.exp(-0.3 * l)
            o, oc = even_mixer(h, hc, even_w_in[e], even_w_out[e], diff_qk_gain[e], diff_lambda[e],
                               diff_subln[e], lam_init, gdn_conv[e], gdn_a_log[e], gdn_dt_bias[e],
                               gdn_norm[e], cos, sin, ctx_out)
        else:
            od = l // 2
            o, oc = odd_mixer(h, hc, odd_w_in[od], odd_w_out[od], na_qk_gain[od], na_rpb[od], ctx_out)
        x = x + g_m * o
        hf = rms_norm(x, norm_ffn[l]) * (1.0 + sc_f) + sh_f
        x = x + g_f * swiglu(hf, ffn_w_in[l], ffn_w_out[l])
        if ctx_out:
            ctx = ctx + cg_m * oc
            hcf = rms_norm(ctx, norm_ffn[l]) * (1.0 + csc_f) + csh_f
            ctx = ctx + cg_f * swiglu(hcf, ffn_w_in[l], ffn_w_out[l])
    return x


N_META = 16
MIX_WIDTH = D_MODEL
FOX_WIDTH = MIX_WIDTH // 2
RET_WIDTH = MIX_WIDTH - FOX_WIDTH
FOX_HEAD_DIM = 64
FOX_HEADS = FOX_WIDTH // FOX_HEAD_DIM
RET_HEADS = 4
RET_HEAD_DIM = RET_WIDTH // RET_HEADS
D_FF = -(-8 * D_MODEL // (3 * 256)) * 256
BLOCK_Q = 128
RET_CHUNK = 128
FGATE_BIAS_MEAN = 3.0
RET_LOG_GAMMA = tuple(math.log(1.0 - 2.0 ** (-5 - h)) for h in range(RET_HEADS))
IN_SIZES = (FOX_WIDTH, FOX_WIDTH, FOX_WIDTH, FOX_HEADS, RET_WIDTH, RET_WIDTH, RET_WIDTH, RET_WIDTH)
IN_COLS = sum(IN_SIZES)
SPLIT_POINTS = tuple(int(v) for v in np.cumsum(IN_SIZES)[:-1])


def rmsnorm(x, g):
    x32 = x.astype(jnp.float32)
    y = x32 * lax.rsqrt(jnp.mean(x32 * x32, axis=-1, keepdims=True) + EPS)
    return (y * g.astype(jnp.float32)).astype(x.dtype)

def rotate(x, cos, sin):
    half = x.shape[-1] // 2
    x1, x2 = x[..., :half], x[..., half:]
    c = cos[None, :, None, :].astype(x.dtype)
    s = sin[None, :, None, :].astype(x.dtype)
    return jnp.concatenate([x1 * c - x2 * s, x1 * s + x2 * c], axis=-1)

def fox_attention(q, k, v, logf):
    B, L, H, Dh = q.shape
    scale = Dh ** -0.5
    c = jnp.cumsum(logf, axis=1).transpose(0, 2, 1)
    qh = q.transpose(0, 2, 1, 3)
    kh = k.transpose(0, 2, 1, 3)
    vh = v.transpose(0, 2, 1, 3)
    pos = jnp.arange(L)

    def attend(q_blk, c_q, q_pos, k_, v_, c_k, k_pos):
        s = jnp.einsum('bhqd,bhkd->bhqk', q_blk, k_).astype(jnp.float32) * scale
        s = s + c_q[..., :, None] - c_k[..., None, :]
        s = jnp.where(k_pos[None, :] <= q_pos[:, None], s, -jnp.inf)
        p = jax.nn.softmax(s, axis=-1)
        return jnp.einsum('bhqk,bhkd->bhqd', p.astype(v_.dtype), v_)

    meta_out = attend(qh[:, :, :N_META], c[:, :, :N_META], pos[:N_META],
                      kh[:, :, :N_META], vh[:, :, :N_META], c[:, :, :N_META], pos[:N_META])
    n_blk = (L - N_META) // BLOCK_Q
    q_real = qh[:, :, N_META:].reshape(B, H, n_blk, BLOCK_Q, Dh).transpose(2, 0, 1, 3, 4)
    c_real = c[:, :, N_META:].reshape(B, H, n_blk, BLOCK_Q).transpose(2, 0, 1, 3)
    pos_real = pos[N_META:].reshape(n_blk, BLOCK_Q)
    real_out = lax.map(lambda a: attend(a[0], a[1], a[2], kh, vh, c, pos),
                       (q_real, c_real, pos_real))
    real_out = real_out.transpose(1, 2, 0, 3, 4).reshape(B, H, L - N_META, Dh)
    out = jnp.concatenate([meta_out, real_out], axis=2)
    return out.transpose(0, 2, 1, 3)

def retention_chunkwise(q, k, v):
    B, L, H, Dh = q.shape
    log_g = jnp.array(RET_LOG_GAMMA, dtype=jnp.float32)

    def intra(qc, kc, vc, n):
        idx = jnp.arange(n)
        diff = idx[:, None] - idx[None, :]
        dec = jnp.where(diff >= 0,
                        jnp.exp(jnp.maximum(diff, 0)[None].astype(jnp.float32) * log_g[:, None, None]),
                        0.0)
        s = jnp.einsum('bnhd,bmhd->bhnm', qc, kc).astype(jnp.float32) * dec
        return jnp.einsum('bhnm,bmhd->bnhd', s, vc.astype(jnp.float32))

    qm, km, vm = q[:, :N_META], k[:, :N_META], v[:, :N_META]
    o_meta = intra(qm, km, vm, N_META)
    m_idx = jnp.arange(N_META, dtype=jnp.float32)
    k_dec_meta = jnp.exp((N_META - 1 - m_idx)[:, None] * log_g[None, :])
    state0 = jnp.einsum('bmhd,bmhe->bhde', km.astype(jnp.float32) * k_dec_meta[None, :, :, None],
                        vm.astype(jnp.float32))

    C = RET_CHUNK
    n_chunks = (L - N_META) // C
    j_idx = jnp.arange(C, dtype=jnp.float32)
    q_dec = jnp.exp((j_idx + 1.0)[:, None] * log_g[None, :])[None, :, :, None]
    k_dec = jnp.exp((C - 1.0 - j_idx)[:, None] * log_g[None, :])[None, :, :, None]
    chunk_dec = jnp.exp(C * log_g)[None, :, None, None]

    def to_chunks(t):
        return t[:, N_META:].reshape(B, n_chunks, C, H, Dh).transpose(1, 0, 2, 3, 4)

    def step(state, xs):
        qc, kc, vc = xs
        o = intra(qc, kc, vc, C) + jnp.einsum('bjhd,bhde->bjhe', qc.astype(jnp.float32) * q_dec, state)
        state = chunk_dec * state + jnp.einsum('bjhd,bjhe->bhde', kc.astype(jnp.float32) * k_dec,
                                               vc.astype(jnp.float32))
        return state, o

    _, o_real = lax.scan(step, state0, (to_chunks(q), to_chunks(k), to_chunks(v)))
    o_real = o_real.transpose(1, 0, 2, 3, 4).reshape(B, L - N_META, H, Dh)
    return jnp.concatenate([o_meta, o_real], axis=1)

def head_groupnorm(o, g):
    mu = jnp.mean(o, axis=-1, keepdims=True)
    var = jnp.mean(jnp.square(o - mu), axis=-1, keepdims=True)
    y = (o - mu) * lax.rsqrt(var + EPS)
    B, L, H, Dh = o.shape
    return y.reshape(B, L, H * Dh) * g.astype(jnp.float32)

def hybrid_layer(h, attn_norm_g, w_in, b_fgate, ret_gn_g, w_out,
                 ffn_norm_g, w_gate, w_up, w_down, cos, sin):
    B, L, _ = h.shape
    xn = rmsnorm(h, attn_norm_g)
    proj = jnp.einsum('bld,dc->blc', xn, w_in)
    fq, fk, fv, flog, rq, rk, rv, rg = jnp.split(proj, SPLIT_POINTS, axis=-1)

    logf = jax.nn.log_sigmoid(flog.astype(jnp.float32) + b_fgate.astype(jnp.float32))
    fshape = (B, L, FOX_HEADS, FOX_HEAD_DIM)
    fox_out = fox_attention(fq.reshape(fshape), fk.reshape(fshape), fv.reshape(fshape), logf)
    fox_out = fox_out.reshape(B, L, FOX_WIDTH)

    rshape = (B, L, RET_HEADS, RET_HEAD_DIM)
    rq_ = rotate(rq.reshape(rshape), cos, sin)
    rk_ = rotate(rk.reshape(rshape), cos, sin) * (RET_HEAD_DIM ** -0.5)
    ret = retention_chunkwise(rq_, rk_, rv.reshape(rshape))
    ret = head_groupnorm(ret, ret_gn_g).astype(h.dtype)
    ret_out = jax.nn.silu(rg) * ret

    mix = jnp.concatenate([fox_out, ret_out], axis=-1)
    h = h + jnp.einsum('blc,cd->bld', mix, w_out)

    hn = rmsnorm(h, ffn_norm_g)
    ff = jax.nn.silu(jnp.einsum('bld,df->blf', hn, w_gate)) * jnp.einsum('bld,df->blf', hn, w_up)
    return h + jnp.einsum('blf,fd->bld', ff, w_down)

def second_inputs(seed: int = 0) -> dict:
    key = jax.random.key(seed)
    ks = jax.random.split(key, 12)
    f32 = jnp.float32
    x = jax.random.normal(ks[0], (BATCH, SEQ, D_MODEL), f32)
    meta_tokens = jax.random.normal(ks[1], (N_META, D_MODEL), f32)
    attn_norm = 1.0 + 0.02 * jax.random.normal(ks[2], (DEPTH, D_MODEL), f32)
    w_in = jax.random.normal(ks[3], (DEPTH, D_MODEL, IN_COLS), f32) * D_MODEL ** -0.5
    b_fgate = FGATE_BIAS_MEAN + 0.5 * jax.random.normal(ks[4], (DEPTH, FOX_HEADS), f32)
    ret_gn = 1.0 + 0.02 * jax.random.normal(ks[5], (DEPTH, RET_WIDTH), f32)
    w_out = jax.random.normal(ks[6], (DEPTH, MIX_WIDTH, D_MODEL), f32) * MIX_WIDTH ** -0.5
    ffn_norm = 1.0 + 0.02 * jax.random.normal(ks[7], (DEPTH, D_MODEL), f32)
    w_gate = jax.random.normal(ks[8], (DEPTH, D_MODEL, D_FF), f32) * D_MODEL ** -0.5
    w_up = jax.random.normal(ks[9], (DEPTH, D_MODEL, D_FF), f32) * D_MODEL ** -0.5
    w_down = jax.random.normal(ks[10], (DEPTH, D_FF, D_MODEL), f32) * D_FF ** -0.5
    final_norm = 1.0 + 0.02 * jax.random.normal(ks[11], (D_MODEL,), f32)
    return {"x": x, "meta_tokens": meta_tokens, "attn_norm": attn_norm, "w_in": w_in,
            "b_fgate": b_fgate, "ret_gn": ret_gn, "w_out": w_out, "ffn_norm": ffn_norm,
            "w_gate": w_gate, "w_up": w_up, "w_down": w_down, "final_norm": final_norm}

def second_block(x, meta_tokens, attn_norm, w_in, b_fgate, ret_gn, w_out, ffn_norm,
              w_gate, w_up, w_down, final_norm):
    B = x.shape[0]
    meta = jnp.broadcast_to(meta_tokens[None].astype(x.dtype), (B, N_META, D_MODEL))
    h = jnp.concatenate([meta, x], axis=1)
    L = h.shape[1]
    inv_freq = ROPE_BASE ** (-jnp.arange(0, RET_HEAD_DIM, 2, dtype=jnp.float32) / RET_HEAD_DIM)
    ang = jnp.arange(L, dtype=jnp.float32)[:, None] * inv_freq[None, :]
    cos, sin = jnp.cos(ang), jnp.sin(ang)
    for i in range(DEPTH):
        h = hybrid_layer(h, attn_norm[i], w_in[i], b_fgate[i], ret_gn[i], w_out[i],
                         ffn_norm[i], w_gate[i], w_up[i], w_down[i], cos, sin)
    h = rmsnorm(h, final_norm)
    return h[:, N_META:]


def setup_inputs(seed=0):
    out = dict(first_inputs(seed))
    for name, value in second_inputs(seed + 1).items():
        if name != "x":
            out[name + "_2"] = value
    return out


def reference(
    x, c, ctx, c_ctx, ada_w, ada_b, norm_mix, norm_ffn, ffn_w_in, ffn_w_out, even_w_in,
    even_w_out, diff_qk_gain, diff_lambda, diff_subln, gdn_conv, gdn_a_log, gdn_dt_bias,
    gdn_norm, odd_w_in, odd_w_out, na_qk_gain, na_rpb, meta_tokens_2, attn_norm_2, w_in_2,
    b_fgate_2, ret_gn_2, w_out_2, ffn_norm_2, w_gate_2, w_up_2, w_down_2, final_norm_2,
):
    x = first_block(
        x, c, ctx, c_ctx, ada_w, ada_b, norm_mix, norm_ffn, ffn_w_in, ffn_w_out, even_w_in,
        even_w_out, diff_qk_gain, diff_lambda, diff_subln, gdn_conv, gdn_a_log, gdn_dt_bias,
        gdn_norm, odd_w_in, odd_w_out, na_qk_gain, na_rpb,
    )
    return second_block(
        x, meta_tokens_2, attn_norm_2, w_in_2, b_fgate_2, ret_gn_2, w_out_2, ffn_norm_2,
        w_gate_2, w_up_2, w_down_2, final_norm_2,
    )


_drawn_inputs = setup_inputs


def setup_inputs(seed=0):
    import zlib

    import numpy as np

    out = dict(_drawn_inputs(seed))
    spreads = {}
    factors = {'norm_mix': 6.694,
     'norm_ffn': 4.158,
     'diff_qk_gain': 8.0,
     'diff_lambda': 8.0,
     'diff_subln': 37.632,
     'gdn_norm': 8.0,
     'na_qk_gain': 8.0,
     'na_rpb': 64.0,
     'ret_gn_2': 39.976,
     'ffn_norm_2': 8.61,
     'attn_norm_2': 4.536,
     'b_fgate_2': 60.696,
     'final_norm_2': 2.67}
    for name, (base, spread) in spreads.items():
        noise = np.random.default_rng([zlib.crc32(name.encode()), seed]).standard_normal(out[name].shape)
        drawn = base * np.exp(spread * noise) if base else spread * noise
        out[name] = __import__('jax').numpy.asarray(drawn.astype(out[name].dtype))
    for name, factor in factors.items():
        out[name] = (out[name] * factor).astype(out[name].dtype)
    return out
```

```python
import math
from contextlib import ExitStack

import concourse.bass as bass
from concourse import mybir
import numpy as np

F32 = mybir.dt.float32
ACT = mybir.ActivationFunctionType
ALU = mybir.AluOpType
AX = mybir.AxisListType

P = 128
D = 1024
KD = D // P
CTX, LAT, META = 256, 512, 16
T = CTX + LAT
TOK2 = CTX - META
T2 = META + LAT
EPS = 1e-6
FF = 2816
FK = FF // P
SLOTS = 4
SLOT_K = 11
BOTH = [(0, CTX), (CTX, LAT)]
LATENT = [(CTX, LAT)]
SECOND = [(TOK2, T2 // 2), (TOK2 + T2 // 2, T2 // 2)]
H4 = 4
GW = 774
NCH = T // P
CH_COL = [2, 2 + P, 260, 260 + P, 260 + 2 * P, 260 + 3 * P]
FWD = [0, 1, 2, 3, 4, 5]
BWD = [1, 0, 5, 4, 3, 2]
LEVELS = 7
RET_LOG_GAMMA = [math.log(1.0 - 2.0 ** (-5 - h)) for h in range(4)]
BIG = 1e30

VEC = {}
_at = 0
for _name, _n in (("norm_mix", 16), ("norm_ffn", 16), ("attn_norm", 16), ("ffn_norm2", 16), ("final", 8),
                  ("diff_gain", 2), ("subln", 1), ("gdn_norm", 1), ("conv", 60), ("na_gain", 2),
                  ("ret_gn", 8), ("ada_b", 96), ("b_fgate", 2), ("c", 16),
                  ("dt_bias", 8), ("a_log", 8), ("lam", 256)):
    VEC[_name] = _at
    _at += _n
NVEC = _at

A_QK = 0
A_GD = 8 * T
A_V = A_GD + 16 * GW
A_SIZE = 24576
A_Q1, A_K1, A_V1, A_BT = 0, 8 * LAT, 8 * LAT + 8 * T, FK * T
NPA = 1056
NPB = 18 * P


class Tally(dict):

    def at(self, name):
        return self.get(name, 0)

    def add(self, name, k=1):
        self[name] = self.get(name, 0) + k
        return self[name]


def shape_tables():
    i = np.arange(P)
    r, c = i[:, None], i[None, :]
    ident = np.eye(P)
    bo64 = (r // 64 == c // 64).astype(np.float64)
    cmask = np.zeros((P, 64))
    q = i % 64
    start = np.clip(q - 8, 0, 48)
    kk = np.arange(64)[None, :]
    cmask[:] = np.where((kk >= start[:, None]) & (kk < start[:, None] + 16), 0.0, -BIG)
    band = np.zeros((P, 128))
    n = np.arange(127)
    for j in range(31):
        band[j, :127] = (78 - n == j)
    dmask = np.where(c <= r, 0.0, -BIG)
    base = np.concatenate([ident, np.ones((P, P)), bo64, cmask, band, dmask], 1)

    inv = 10000.0 ** (-np.arange(16, dtype=np.float32) / np.float32(16))
    t = np.arange(LAT)
    ang = np.concatenate([(t // 64).astype(np.float32)[:, None] * inv, (t % 64).astype(np.float32)[:, None] * inv], 1)
    f = (i % 64) // 2
    cos1 = np.cos(ang)[:, f].T
    sin1 = np.sin(ang)[:, f].T * np.where(i % 2 == 0, -1.0, 1.0)[:, None]
    rope1 = np.concatenate([cos1, sin1, np.zeros((P, NPA - 2 * LAT))], 1)
    inv2 = 10000.0 ** (-np.arange(0, 128, 2, dtype=np.float32) / np.float32(128))
    ang2 = np.arange(T2, dtype=np.float32)[:, None] * inv2[None]
    cos2 = np.cos(ang2)[:, i % 64].T
    sin2 = np.sin(ang2)[:, i % 64].T * np.where(i < 64, -1.0, 1.0)[:, None]
    rope2 = np.concatenate([cos2, sin2], 1)

    mats = [(r > c), (r < c), (r <= c), (r >= c)]
    for lv in range(LEVELS):
        same = (r >> (lv + 1)) == (c >> (lv + 1))
        rb, cb = (r >> lv) & 1, (c >> lv) & 1
        mats += [same & (rb == 0) & (cb == 1), same & (rb == 1) & (cb == 0)]
    masks = np.concatenate([m.astype(np.float64) for m in mats], 1)
    lg = np.array(RET_LOG_GAMMA)
    s, tt = r, c
    dec = [np.where(tt >= s, np.exp(np.maximum(tt - s, 0) * lg[h]), 0.0) for h in range(4)]
    qd = [np.broadcast_to(np.exp((i + 1.0) * lg[h])[None], (P, P)) for h in range(4)]
    kd = np.stack([np.exp((P - 1.0 - i) * lg[h]) for h in range(4)], 1)
    kdm = np.stack([np.exp((META - 1.0 - i) * lg[h]) * (i < META) for h in range(4)], 1)
    hot = np.zeros((P, 1024))
    for h in range(8):
        hot[h, h * P:(h + 1) * P] = -1.0
    ret = np.concatenate(dec + qd + [hot, kd, kdm], 1)
    ret = np.concatenate([ret, np.zeros((P, NPB - ret.shape[1]))], 1)
    out = [np.ascontiguousarray(a, np.float32) for a in (base, rope1, rope2, masks, ret)]
    return dict(zip(("base", "rope1", "rope2", "masks", "ret"), out))


def build(nc, dram, out):
    with ExitStack() as ctx:
        def sb(name, shape):
            return ctx.enter_context(nc.sbuf_tensor(name, shape, F32))

        x = sb("resid", [P, KD, T])
        h = sb("hidden", [P, KD, T])
        mix = h
        ring = sb("ring", [P, SLOTS, SLOT_K * P])
        arena = sb("arena", [P, A_SIZE])
        scr = sb("scr", [P, 6, GW])
        base = sb("base", [P, 3 * P + 64 + 128 + P])
        pa = sb("pa", [P, NPA])
        pb_ = sb("pb", [P, NPB])
        vec = sb("vec", [P, NVEC])
        mod = sb("mod", [P, 96, 2])
        amod = sb("amod", [P, 4, KD, 2])
        csil = sb("csil", [P, KD, 2])
        wsmall = sb("wsmall", [P, KD, 16])
        small = sb("small", [P, 96])
        gates = sb("gates", [P, 8, 48])
        eps_t = sb("eps_t", [P, 1])
        eps_ap = eps_t[:, 0:1]
        ps = ctx.enter_context(nc.psum_tensor("ps", [P, 8, 512], F32))

        names = ("inputs_landed", "tables_landed", "small_landed", "rpb_landed", "meta_landed", "block_done",
                 "tile_read", "gate_ready", "squares_ready", "squares_used",
                 "sums_ready", "roots_ready", "scaled_ready", "modulated", "head_scaled", "swapped",
                 "scores_ready", "bias_ready", "exp_done", "p_ready", "pt_psum", "pt_copied", "pv_done",
                 "o_read", "phase_done", "act_chain", "dve_chain", "pool_chain", "setup_ready",
                 "conv_ready", "conv_used", "bt_ready", "bt_read", "f_logits", "f_z", "f_log", "f_cum", "f_rows",
                 "f_read", "turned", "r_raw", "r_scaled", "r_sums", "r_out", "means", "final_ready", "step_pe", "step_act", "step_dve", "step_pool", "out_ready", "stored")
        s = {n: ctx.enter_context(nc.semaphore(n)) for n in names}
        w_landed = [ctx.enter_context(nc.semaphore(f"w_landed{i}")) for i in range(SLOTS)]

        ident = base[:, 0:P]
        ones = base[:, P:2 * P]
        bo64 = base[:, 2 * P:3 * P]
        cmask = base[:, 3 * P:3 * P + 64]
        band = base[:, 3 * P + 64:3 * P + 64 + 128]
        dmask = base[:, 3 * P + 192:4 * P + 192]

        def v(name, i=0, n=1):
            return vec[:, VEC[name] + i:VEC[name] + i + n]

        def v_at(name, i):
            return vec[:, :].rearrange("p (n o) -> p n o", o=1)[:, VEC[name] + i, :]

        def bc(ap, shape):
            return ap.to_broadcast(shape)

        FULL = KD * P
        stream = [("ada", 24, FULL), ("even_in", 7, FULL), ("even_out", 2, FULL), ("gu0", 11, FULL),
                  ("dn0", 4, SLOT_K * P), ("odd_in", 6, FULL), ("odd_out", 2, FULL), ("gu1", 11, FULL),
                  ("dn1", 4, SLOT_K * P)]
        for l in range(2):
            stream += [(f"in2_{l}", 7, FULL), (f"out2_{l}", 2, FULL), (f"gu2_{l}", 11, FULL),
                       (f"dn2_{l}", 4, SLOT_K * P)]

        block = ctx.enter_context(nc.Block())

        def end_phase(eng, n):
            eng.drain().then_inc(s["phase_done"], 1)
            eng.wait_ge(s["phase_done"], 4 * n.add("phase"))

        @block.sync
        def _(sp):
            sp.dma_start(vec[:, :], dram["vecs"]).then_inc(s["inputs_landed"], 16)
            sp.dma_start(base[:, :], dram["base"]).then_inc(s["inputs_landed"], 16)
            sp.dma_start(x[:, :, 0:CTX], dram["ctxT"]).then_inc(s["inputs_landed"], 16)
            sp.dma_start(x[:, :, CTX:T], dram["xT"]).then_inc(s["inputs_landed"], 16)
            done = 0
            for name, turns, cols in stream:
                w = dram[name]
                first = 0
                if done == 0:
                    for j in range(SLOTS):
                        sp.dma_start(ring[:, j, 0:cols], w[j]).then_inc(w_landed[j], 16)
                    first = 1
                with sp.Fori(first, turns) as i:
                    for j in range(SLOTS):
                        sp.wait_ge(s["block_done"], 4 * i + (done + j - 3))
                        sp.dma_start(ring[:, j, 0:cols], w[4 * i + j]).then_inc(w_landed[j], 16)
                done += SLOTS * turns
            sp.wait_ge(s["out_ready"], 4)
            sp.dma_start(out.rearrange("(t p) d -> p t d", p=P), arena[:, 0:4 * D].rearrange("p (t d) -> p t d", t=4)
                         ).then_inc(s["stored"], 16)
            sp.wait_ge(s["stored"], 16)

        def pool_tables(pool, a, b):
            pool.dma_start(pa[:, :], dram[a]).then_inc(s["tables_landed"], 16)
            pool.dma_start(pb_[:, :], dram[b]).then_inc(s["tables_landed"], 16)

        def dve_link(dve, n, ins):
            ins.then_inc(s["dve_chain"], 1)
            dve.wait_ge(s["dve_chain"], n.add("dve_chain"))

        def act_link(act, n, ins):
            ins.then_inc(s["act_chain"], 1)
            act.wait_ge(s["act_chain"], n.add("act_chain"))

        def pe_project(pe, n, acts, halves, turns):
            turn0, read0 = n.at("turn"), n.at("tile_read")
            with pe.Fori(0, turns) as i:
                for j in range(SLOTS):
                    pe.wait_ge(w_landed[j], 16 * i + 16 * (turn0 + 1))
                    pe.wait_ge(s["tile_read"], 4 * i + (read0 + j + 1))
                    for k in range(KD):
                        for b, (c0, cn) in enumerate(halves):
                            mm = pe.matmul(ps[:, 2 * j + b, 0:cn], ring[:, j, k * P:(k + 1) * P],
                                           acts[:, k, c0:c0 + cn], start=(k == 0), stop=(k == KD - 1))
                    mm.then_inc(s["block_done"], 1)

        def pe_project_tok(pe, n, acts, tiles, turns):
            for i in range(turns):
                for j in range(SLOTS):
                    pe.wait_ge(w_landed[j], 16 * (n.at("turn") + i) + 16)
                    pe.wait_ge(s["tile_read"], n.at("tile_read") + SLOTS * i + j + 1)
                    for t, (c0, rows) in enumerate(tiles):
                        for k in range(KD):
                            mm = pe.matmul(ps[0:rows, 2 * j + t // 4, (t % 4) * P:(t % 4 + 1) * P],
                                           acts[:, k, c0:c0 + rows], ring[:, j, k * P:(k + 1) * P],
                                           start=(k == 0), stop=(k == KD - 1))
                    mm.then_inc(s["block_done"], 1)

        def dve_copy_out(dve, n, halves, turns, dst, scale=None):
            b0 = n.at("block_done")
            with dve.Fori(0, turns) as i:
                for j in range(SLOTS):
                    dve.wait_ge(s["block_done"], 4 * i + (b0 + j + 1))
                    for b, (c0, cn) in enumerate(halves):
                        if scale is None:
                            ins = dve.tensor_copy(dst(4 * i + j, b), ps[:, 2 * j + b, 0:cn])
                        else:
                            ins = dve.tensor_scalar(dst(4 * i + j, b), ps[:, 2 * j + b, 0:cn], scale, None, ALU.mult)
                    ins.then_inc(s["tile_read"], 1)

        def dve_copy_tok(dve, n, tiles, turns, dst):
            for i in range(turns):
                for j in range(SLOTS):
                    dve.wait_ge(s["block_done"], n.at("block_done") + SLOTS * i + j + 1)
                    f0 = (SLOTS * i + j) * P
                    src = ps[:, 2 * j:2 * j + 2, :].rearrange("p a b -> p (a b)")
                    full = len(tiles) if tiles[0][1] == P else len(tiles) - 1
                    ins = dve.tensor_copy(dst[:, 0:full, f0:f0 + P],
                                          src[:, 0:full * P].rearrange("p (t f) -> p t f", f=P))
                    if full < len(tiles):
                        rows = tiles[-1][1]
                        ins = dve.tensor_copy(dst[0:rows, full, f0:f0 + P], src[0:rows, full * P:full * P + P])
                    ins.then_inc(s["tile_read"], 1)

        def dve_residual(dve, n, halves, turns, gate, down):
            b0 = n.at("block_done")
            per = 2 if down else SLOTS
            with dve.Fori(0, turns) as i:
                for t in range(per):
                    bank = 4 * t if down else 2 * t
                    dve.wait_ge(s["block_done"], 4 * i + (b0 + (2 * t + 2 if down else t + 1)))
                    m = per * i + t
                    for b, (c0, cn) in enumerate(halves):
                        dst = x[:, m, c0:c0 + cn]
                        if gate is None:
                            ins = dve.tensor_tensor(dst, ps[:, bank + b, 0:cn], dst, ALU.add)
                        else:
                            g = mod[:, gate + m, (1 if c0 == 0 else 0):(2 if c0 == 0 else 1)]
                            ins = dve.scalar_tensor_tensor(dst, ps[:, bank + b, 0:cn], g, dst, ALU.mult, ALU.add)
                    ins.then_inc(s["tile_read"], 1)

        ff = arena[:, 0:FK * T].rearrange("p (m t) -> p m t", m=FK)

        def act_gates(act, n, halves):
            b0, r0 = n.at("block_done"), n.at("tile_read")
            with act.Fori(0, 11) as i:
                for q in range(2):
                    act.wait_ge(s["block_done"], 4 * i + (b0 + 2 * q + 1))
                    act.wait_ge(s["tile_read"], 4 * i + (r0 + 2 * q + 2))
                    for b, (c0, cn) in enumerate(halves):
                        ins = act.activation(scr[:, q, c0:c0 + cn], ps[:, 4 * q + b, 0:cn], ACT.Silu)
                    ins.then_inc(s["gate_ready"], 1)

        def dve_products(dve, n, halves):
            b0, g0 = n.at("block_done"), n.at("gate_ready")
            with dve.Fori(0, 11) as i:
                for q in range(2):
                    dve.wait_ge(s["block_done"], 4 * i + (b0 + 2 * q + 2))
                    dve.wait_ge(s["gate_ready"], 2 * i + (g0 + q + 1))
                    for b, (c0, cn) in enumerate(halves):
                        ins = dve.tensor_tensor(ff[:, 2 * i + q, c0:c0 + cn], scr[:, q, c0:c0 + cn],
                                                ps[:, 4 * q + 2 + b, 0:cn], ALU.mult)
                    ins.then_inc(s["tile_read"], 2)

        def pe_down(pe, n, halves):
            turn0, read0 = n.at("turn"), n.at("tile_read")
            with pe.Fori(0, 4) as i:
                for t in range(2):
                    pe.wait_ge(s["tile_read"], 2 * i + (read0 + t + 3))
                    for q in range(2):
                        j = 2 * t + q
                        pe.wait_ge(w_landed[j], 16 * i + 16 * (turn0 + 1))
                        for k in range(SLOT_K):
                            for b, (c0, cn) in enumerate(halves):
                                mm = pe.matmul(ps[:, 4 * t + b, 0:cn], ring[:, j, k * P:(k + 1) * P],
                                               ff[:, q * SLOT_K + k, c0:c0 + cn],
                                               start=(q == 0 and k == 0), stop=(q == 1 and k == SLOT_K - 1))
                        mm.then_inc(s["block_done"], 1)

        def act_norm(act, n, halves, a, shift):
            c0 = halves[0][0]
            end = halves[-1][0] + halves[-1][1]
            u0 = n.at("squares_used")
            for k in range(KD):
                if k >= 2:
                    act.wait_ge(s["squares_used"], u0 + k - 1)
                act.activation(scr[:, k % 2, c0:end], x[:, k, c0:end], ACT.Square).then_inc(s["squares_ready"], 1)
            act.wait_ge(s["squares_used"], u0 + KD)
            for b, (h0, hn) in enumerate(halves):
                ins = act.activation(scr[:, 2, h0:h0 + hn], ps[:, b, 0:hn], ACT.Sqrt, bias=eps_ap, scale=1.0 / D)
            ins.then_inc(s["roots_ready"], 1)
            if a is not None:
                for k in range(KD):
                    act.wait_ge(s["scaled_ready"], n.at("scaled_ready") + k + 1)
                    for b, (h0, hn) in enumerate(halves):
                        z = 1 if h0 == 0 else 0
                        ins = act.activation(h[:, k, h0:h0 + hn], scr[:, 4 + k % 2, h0:h0 + hn], ACT.Identity,
                                             bias=mod[:, shift + k, z:z + 1], scale=amod[:, a, k, z:z + 1])
                    ins.then_inc(s["modulated"], 1)

        def pe_norm(pe, n, halves):
            for k in range(KD):
                pe.wait_ge(s["squares_ready"], n.at("squares_ready") + k + 1)
                for b, (h0, hn) in enumerate(halves):
                    mm = pe.matmul(ps[:, b, 0:hn], ones, scr[:, k % 2, h0:h0 + hn], start=(k == 0), stop=(k == KD - 1))
                mm.then_inc(s["squares_used"], 1)

        def dve_norm(dve, n, halves, gain):
            c0 = halves[0][0]
            end = halves[-1][0] + halves[-1][1]
            dve.wait_ge(s["roots_ready"], n.at("roots_ready") + 1)
            dve_link(dve, n, dve.reciprocal(scr[:, 3, c0:end], scr[:, 2, c0:end]))
            m0 = n.at("modulated")
            for k in range(KD):
                if gain is None:
                    if k >= 2:
                        dve.wait_ge(s["modulated"], m0 + k - 1)
                    dve.tensor_tensor(scr[:, 4 + k % 2, c0:end], x[:, k, c0:end], scr[:, 3, c0:end],
                                      ALU.mult).then_inc(s["scaled_ready"], 1)
                else:
                    dve.scalar_tensor_tensor(h[:, k, c0:end], x[:, k, c0:end], gain(k), scr[:, 3, c0:end],
                                             ALU.mult, ALU.mult)

        def halves_of(cols):
            return [(0, cols // 2), (cols // 2, cols // 2)] if cols > 512 else [(0, cols)]

        def act_head_norm(act, n, tiles, matrix, scale, rope):
            q0, r0, d0 = n.at("sums_ready"), n.at("roots_ready"), n.at("head_scaled")

            def root(i):
                cols = tiles[i][3]
                act.wait_ge(s["sums_ready"], q0 + i + 1)
                if i >= 2:
                    act.wait_ge(s["head_scaled"], d0 + i - 1)
                for b, (c0, cn) in enumerate(halves_of(cols)):
                    ins = act.activation(scr[:, 2 + i % 2, c0:c0 + cn], ps[:, 2 * (i % 2) + b, 0:cn], ACT.Sqrt,
                                         bias=eps_ap, scale=scale)
                ins.then_inc(s["roots_ready"], 1)

            for i, (src, dst, gain, cols) in enumerate(tiles):
                if i >= 2:
                    act.wait_ge(s["sums_ready"], q0 + i - 1)
                act.activation(scr[:, i % 2, 0:cols], src, ACT.Square).then_inc(s["squares_ready"], 1)
                if i >= 1:
                    root(i - 1)
            root(len(tiles) - 1)

        def pe_head_norm(pe, n, tiles, matrix, scale, rope):
            for i, (src, dst, gain, cols) in enumerate(tiles):
                pe.wait_ge(s["squares_ready"], n.at("squares_ready") + i + 1)
                if i >= 2:
                    pe.wait_ge(s["roots_ready"], n.at("roots_ready") + i - 1)
                for b, (c0, cn) in enumerate(halves_of(cols)):
                    mm = pe.matmul(ps[:, 2 * (i % 2) + b, 0:cn], matrix, scr[:, i % 2, c0:c0 + cn], start=True, stop=True)
                mm.then_inc(s["sums_ready"], 1)

        def dve_head_norm(dve, n, tiles, matrix, scale, rope):
            for i, (src, dst, gain, cols) in enumerate(tiles):
                dve.wait_ge(s["roots_ready"], n.at("roots_ready") + i + 1)
                r = scr[:, 2 + i % 2, 0:cols]
                dve_link(dve, n, dve.reciprocal(r, r))
                ins = dve.scalar_tensor_tensor(dst, src, gain, r, ALU.mult, ALU.mult)
                ins.then_inc(s["head_scaled"], 1)
                if rope:
                    y = dst[:, CTX:T] if cols == T else dst
                    dve.wait_ge(s["head_scaled"], n.at("head_scaled") + i + 1)
                    dve_link(dve, n, dve.stream_shuffle(scr[:, 4, 0:LAT], y, [j ^ 1 for j in range(32)]))
                    dve.tensor_tensor(scr[:, 5, 0:LAT], y, pa[:, 0:LAT], ALU.mult)
                    dve_link(dve, n, dve.tensor_tensor(scr[:, 4, 0:LAT], scr[:, 4, 0:LAT], pa[:, LAT:2 * LAT], ALU.mult))
                    dve_link(dve, n, dve.tensor_tensor(y, scr[:, 4, 0:LAT], scr[:, 5, 0:LAT], ALU.add))

        def score_banks(m, u, maps):
            return 2 * (m if maps == 2 else u % 2)

        def pe_attend(pe, n, units, maps, bias):
            U = len(units)

            def scores(u):
                w = units[u]
                for m in range(maps):
                    g = u * maps + m
                    if g >= 2:
                        name = "bias_ready" if bias else "exp_done"
                        pe.wait_ge(s[name], n.at(name) + g - 1)
                    for b, k0, kn in w["segs"]:
                        mm = pe.matmul(ps[0:w["nq"], score_banks(m, u, maps) + b, 0:kn], w["q"][m], w["k"][m][:, k0:k0 + kn],
                                       start=True, stop=True)
                    mm.then_inc(s["scores_ready"], 1)

            def turn(u):
                w = units[u]
                pe.wait_ge(s["p_ready"], n.at("p_ready") + u + 1)
                if u >= 1:
                    pe.wait_ge(s["pt_copied"], n.at("pt_copied") + u)
                for t, (c0, rows) in enumerate(w["keys"]):
                    src = scr[0:w["nq"], w["p"], c0:c0 + rows]
                    mm = pe.transpose(ps[0:rows, 4 + t // 4, (t % 4) * P:(t % 4) * P + w["nq"]], src,
                                      ident[0:w["nq"], 0:w["nq"]])
                mm.then_inc(s["pt_psum"], 1)

            def weigh(u):
                w = units[u]
                pe.wait_ge(s["pt_copied"], n.at("pt_copied") + u + 1)
                if u >= 2:
                    pe.wait_ge(s["o_read"], n.at("o_read") + u - 1)
                o0, on = w["o_part"]
                for t, (c0, rows) in enumerate(w["keys"]):
                    mm = pe.matmul(ps[o0:o0 + on, 6 + u % 2, 0:w["nq"]], w["v"][t],
                                   scr[0:rows, 4 + u % 2, t * P:t * P + w["nq"]],
                                   start=(t == 0), stop=(t == len(w["keys"]) - 1))
                mm.then_inc(s["pv_done"], 1)

            for st in range(U + 2):
                if st < U:
                    scores(st)
                if 1 <= st <= U:
                    turn(st - 1)
                if st >= 2:
                    weigh(st - 2)

        def act_attend(act, n, units, maps, bias):
            U = len(units)
            for st in range(U + 1):
                if st < U:
                    w = units[st]
                    for m in range(maps):
                        g = st * maps + m
                        act.wait_ge(s["bias_ready"], n.at("bias_ready") + g + 1)
                        if bias:
                            z = scr[0:w["nq"], w["p"], 0:w["nk"]]
                            src = z
                        else:
                            z = scr[0:w["nq"], m, 0:w["nk"]]
                            c = w["segs"][0][2]
                            src = ps[0:w["nq"], 2 * m:2 * m + 2, 0:c]
                            z = z.rearrange("p (a b) -> p a b", a=2)
                            if st >= 1:
                                act.wait_ge(s["p_ready"], n.at("p_ready") + st)
                        act.activation(z, src, ACT.Exp, bias=small[0:w["nq"], g % 4:g % 4 + 1], scale=1.0,
                                       accum_out=small[0:w["nq"], 4 + g % 4:5 + g % 4]).then_inc(s["exp_done"], 1)
                if st >= 1:
                    u = st - 1
                    w = units[u]
                    act.wait_ge(s["pt_psum"], n.at("pt_psum") + u + 1)
                    if u >= 2:
                        act.wait_ge(s["pv_done"], n.at("pv_done") + u - 1)
                    nt, nq = len(w["keys"]), w["nq"]
                    whole = [t for t in range(nt) if w["keys"][t][1] == P]
                    for bank in (0, 1):
                        ts = [t for t in whole if t // 4 == bank]
                        if ts:
                            a, z = ts[0], ts[-1] + 1
                            ins = act.copy(scr[:, 4 + u % 2, a * P:z * P].rearrange("p (t q) -> p t q", q=P)[:, :, 0:nq],
                                           ps[:, 4 + bank, (a % 4) * P:(a % 4 + z - a) * P].rearrange(
                                               "p (t q) -> p t q", q=P)[:, :, 0:nq])
                    for t in range(nt):
                        rows = w["keys"][t][1]
                        if rows != P:
                            ins = act.copy(scr[0:rows, 4 + u % 2, t * P:t * P + nq],
                                           ps[0:rows, 4 + t // 4, (t % 4) * P:(t % 4) * P + nq])
                    ins.then_inc(s["pt_copied"], 1)

        def dve_attend(dve, n, units, maps, bias):
            U = len(units)

            def shift(u):
                w = units[u]
                nq = w["nq"]
                for m in range(maps):
                    g = u * maps + m
                    dve.wait_ge(s["scores_ready"], n.at("scores_ready") + g + 1)
                    top = small[0:nq, g % 4:g % 4 + 1]
                    if not bias:
                        c = w["segs"][0][2]
                        dve.tensor_reduce(top, ps[0:nq, 2 * m:2 * m + 2, 0:c], AX.XY, ALU.max, negate=True
                                          ).then_inc(s["bias_ready"], 1)
                        continue
                    if u >= 2:
                        dve.wait_ge(s["pt_psum"], n.at("pt_psum") + u - 1)
                    z = scr[0:nq, w["p"], 0:w["nk"]]
                    for b, k0, kn in w["segs"]:
                        src = ps[0:nq, 2 * (u % 2) + b, 0:kn]
                        kind, arg = w["bias"][b]
                        if kind == "plain":
                            ins = dve.tensor_copy(z[:, k0:k0 + kn], src)
                        elif kind == "table":
                            ins = dve.tensor_tensor(z[:, k0:k0 + kn], src, arg, ALU.add)
                        else:
                            ins = dve.scalar_tensor_tensor(z[:, k0:k0 + kn], src, arg[0], arg[1][:, k0:k0 + kn],
                                                           ALU.add, ALU.add)
                    dve_link(dve, n, ins)
                    if w["diag"] is not None:
                        d = z[:, w["diag"]:w["diag"] + nq]
                        dve_link(dve, n, dve.tensor_tensor(d, d, dmask[0:nq, 0:nq], ALU.add))
                    dve.tensor_reduce(top, z, AX.X, ALU.max, negate=True).then_inc(s["bias_ready"], 1)

            def normalise(u):
                w = units[u]
                nq = w["nq"]
                dve.wait_ge(s["exp_done"], n.at("exp_done") + maps * (u + 1))
                g = u * maps
                sums = small[0:nq, 4 + g % 4:4 + g % 4 + maps]
                inv = small[0:nq, 8 + 2 * (u % 2):8 + 2 * (u % 2) + maps]
                both = small[0:nq, 12 + u % 2:13 + u % 2]
                dve_link(dve, n, dve.reciprocal(inv, sums))
                z = scr[0:nq, w["p"], 0:w["nk"]]
                if maps == 1:
                    dve.tensor_scalar(z, z, inv[:, 0:1], None, ALU.mult).then_inc(s["p_ready"], 1)
                    return
                if u >= 2:
                    dve.wait_ge(s["pt_psum"], n.at("pt_psum") + u - 1)
                dve.tensor_scalar(z, scr[0:nq, 0, 0:w["nk"]], inv[:, 0:1], None, ALU.mult).then_inc(s["dve_chain"], 1)
                dve.tensor_tensor(both, inv[:, 1:2], small[0:nq, 16:17], ALU.mult).then_inc(s["dve_chain"], 1)
                dve.wait_ge(s["dve_chain"], n.add("dve_chain", 2))
                dve.scalar_tensor_tensor(z, scr[0:nq, 1, 0:w["nk"]], both, z, ALU.mult, ALU.add
                                         ).then_inc(s["p_ready"], 1)

            def take(u):
                w = units[u]
                o0, on = w["o_part"]
                dve.wait_ge(s["pv_done"], n.at("pv_done") + u + 1)
                dve.tensor_copy(w["out"], ps[o0:o0 + on, 6 + u % 2, 0:w["nq"]]).then_inc(s["o_read"], 1)

            for st in range(U + 3):
                if st < U:
                    shift(st)
                if 1 <= st <= U:
                    normalise(st - 1)
                if 3 <= st:
                    take(st - 3)

        def act_setup(act, n):
            act.wait_ge(s["inputs_landed"], 64)
            act.sem_inc(s["tile_read"], 4)
            act_link(act, n, act.activation(csil[:, :, :], v("c", 0, 16).rearrange("p (k z) -> p k z", k=KD), ACT.Silu))
            act.wait_ge(s["setup_ready"], 1)
            act.activation(small[:, 18:20], small[:, 18:20], ACT.Exp).then_inc(s["setup_ready"], 1)

        def dve_setup(dve, n):
            dve.wait_ge(s["inputs_landed"], 64)
            dve.memset(eps_t[:, :], EPS)
            dve.memset(small[:, 20:96], 0.0)
            for c in (0, 2 + CTX, GW - 2):
                dve.memset(gd[:, :, c:c + 2], 0.0)
            lam = v("lam", 0, 256).rearrange("p (a d) -> p a d", a=4)
            prod = scr[:, 0, 0:128].rearrange("p (a d) -> p a d", a=2)
            dve_link(dve, n, dve.tensor_tensor(prod[:, 0:1, :], lam[:, 0:1, :], lam[:, 1:2, :], ALU.mult))
            dve_link(dve, n, dve.tensor_tensor(prod[:, 1:2, :], lam[:, 2:3, :], lam[:, 3:4, :], ALU.mult))
            dve.tensor_reduce(small[:, 18:20], prod, AX.X, ALU.add).then_inc(s["setup_ready"], 1)
            dve.wait_ge(s["setup_ready"], 2)
            dve_link(dve, n, dve.tensor_tensor(small[:, 16:17], small[:, 19:20], small[:, 18:19], ALU.subtract))
            dve_link(dve, n, dve.tensor_scalar(small[:, 16:17], small[:, 16:17], -LAM_INIT, None, ALU.add))
            dve.tensor_scalar(v("diff_gain"), v("diff_gain"), 64 ** -0.5, None, ALU.mult)
            dve.tensor_scalar(v("na_gain"), v("na_gain"), 128 ** -0.5, None, ALU.mult)
            dve.tensor_scalar(v("subln"), v("subln"), 1.0 - LAM_INIT, None, ALU.mult)

        LAM_INIT = 0.8 - 0.6 * math.exp(0.0)

        def pe_ada(pe, n):
            pe.wait_ge(s["act_chain"], 1)
            with pe.Fori(0, 24) as i:
                for j in range(SLOTS):
                    pe.wait_ge(w_landed[j], 16 * i + 16)
                    pe.wait_ge(s["tile_read"], 4 * i + (j + 1))
                    for k in range(KD):
                        mm = pe.matmul(ps[:, 2 * j, 0:2], ring[:, j, k * P:(k + 1) * P], csil[:, k, :],
                                       start=(k == 0), stop=(k == KD - 1))
                    mm.then_inc(s["block_done"], 1)

        def dve_ada(dve, n):
            with dve.Fori(0, 24) as i:
                for j in range(SLOTS):
                    dve.wait_ge(s["block_done"], 4 * i + (j + 1))
                    dve.tensor_scalar(mod[:, 4 * i + j, :], ps[:, 2 * j, 0:2], v_at("ada_b", 4 * i + j), None, ALU.add
                                      ).then_inc(s["tile_read"], 1)
            dve.wait_ge(s["tile_read"], 4 + 96)
            for l in range(2):
                for f, name in ((0, "norm_mix"), (1, "norm_ffn")):
                    sc = mod[:, 48 * l + 24 * f + 8:48 * l + 24 * f + 16, :]
                    g = v(name, 8 * l, 8).unsqueeze(2).to_broadcast([P, KD, 2])
                    dve.scalar_tensor_tensor(amod[:, 2 * l + f, :, :], sc, 1.0, g, ALU.add, ALU.mult)

        gd = arena[:, A_GD:A_GD + 16 * GW].rearrange("p (m t) -> p m t", m=16)
        GN = GW - 4

        def dve_conv(dve, n):
            for m in range(12):
                acc = scr[:, 4 + m % 2, 0:GN]
                if m >= 2:
                    dve.wait_ge(s["conv_used"], m - 1)
                w = lambda j: v("conv", 5 * m + j)
                dve_link(dve, n, dve.tensor_scalar(acc, gd[:, m, 0:GN], w(0), None, ALU.mult))
                for j in range(1, 5):
                    ins = dve.scalar_tensor_tensor(acc, gd[:, m, j:j + GN], w(j), acc, ALU.mult, ALU.add)
                    if j < 4:
                        dve_link(dve, n, ins)
                ins.then_inc(s["conv_ready"], 1)

        def act_conv(act, n):
            for m in range(12):
                act.wait_ge(s["conv_ready"], m + 1)
                act.activation(gd[:, m, 2:2 + CTX], scr[:, 4 + m % 2, 0:CTX], ACT.Silu)
                act.activation(gd[:, m, 260:260 + LAT], scr[:, 4 + m % 2, 258:258 + LAT], ACT.Silu
                               ).then_inc(s["conv_used"], 1)

        la = gates[:, 0]
        beta = gates[:, 1]
        egrt = gates[:, 2:5]
        kscale = gates[:, 5]

        def by_dir(tab):
            return tab.rearrange("p (s d h) -> p d s h", s=6, d=2)

        def step_bc(tab, st):
            return tab[:, 8 * st:8 * st + 8].unsqueeze(2).to_broadcast([P, 8, P])

        def pe_gates_raw(pe, n):
            pe.wait_ge(s["small_landed"], 16)
            for c in range(NCH):
                for k in range(KD):
                    mm = pe.matmul(ps[:, 0, 16 * c:16 * c + 16], h[:, k, c * P:(c + 1) * P], wsmall[:, k, :],
                                   start=(k == 0), stop=(k == KD - 1))
            mm.then_inc(s["step_pe"], 1)

        def dve_gates_raw(dve, n):
            dve.wait_ge(s["step_pe"], 1)
            for st in range(6):
                for d, c in ((0, FWD[st]), (1, BWD[st])):
                    o = 8 * st + 4 * d
                    dve.tensor_copy(beta[:, o:o + 4], ps[:, 0, 16 * c + 4 * d:16 * c + 4 * d + 4])
                    dve.tensor_copy(la[:, o:o + 4], ps[:, 0, 16 * c + 8 + 4 * d:16 * c + 8 + 4 * d + 4])

        def dve_gates(dve, n):
            t0, t1 = gates[:, 6], gates[:, 7]
            shp = [P, 6, 8]
            cube = lambda a: a.rearrange("p (s e) -> p s e", e=8)
            dve.tensor_tensor(cube(la), cube(la), v("dt_bias", 0, 8).unsqueeze(1).to_broadcast(shp), ALU.add
                              ).then_inc(s["step_dve"], 1)
            dve.wait_ge(s["step_act"], 2)
            dve_link(dve, n, dve.tensor_scalar(beta, beta, 1.0, None, ALU.add))
            dve_link(dve, n, dve.reciprocal(beta, beta))
            dve_link(dve, n, dve.scalar_tensor_tensor(la, la, 0.0, t0, ALU.max, ALU.add))
            dve.scalar_tensor_tensor(cube(la), cube(la), -1.0, small[:, 20:28].unsqueeze(1).to_broadcast(shp),
                                     ALU.mult, ALU.mult).then_inc(s["step_dve"], 1)
            dve.wait_ge(s["step_act"], 3)
            dve.tensor_tensor(kscale, beta, gates[:, 3], ALU.mult)

        def act_gates_tab(act, n):
            t0 = gates[:, 6]
            act.activation(beta, beta, ACT.Exp, scale=-1.0)
            act.activation(small[:, 20:28], v("a_log", 0, 8), ACT.Exp)
            act.wait_ge(s["step_dve"], 1)
            act_link(act, n, act.activation(t0, la, ACT.Abs))
            act_link(act, n, act.activation(t0, t0, ACT.Exp, scale=-1.0))
            act.activation(t0, t0, ACT.Ln, bias=1.0).then_inc(s["step_act"], 2)
            act.wait_ge(s["step_pe"], 2)
            act.activation(gates[:, 2:5].rearrange("p a (s d h) -> p a d s h", s=6, d=2)[:, 0], ps[:, 0, 0:48].rearrange("p (d s h) -> p d s h", d=2, s=6), ACT.Exp)
            act.activation(gates[:, 3].rearrange("p (s d h) -> p d s h", s=6, d=2), ps[:, 0, 48:96].rearrange("p (d s h) -> p d s h", d=2, s=6), ACT.Exp)
            act.activation(gates[:, 4].rearrange("p (s d h) -> p d s h", s=6, d=2), ps[:, 0, 96:144].rearrange("p (d s h) -> p d s h", d=2, s=6), ACT.Exp
                           ).then_inc(s["step_act"], 1)

        def pe_gates_tab(pe, n):
            pe.wait_ge(s["step_dve"], 2)
            for d in range(2):
                r = by_dir(la)[:, d]
                for kind, m in ((0, mask(2 + d)), (1, mask(d)), (2, ones)):
                    mm = pe.matmul(ps[:, 0, 48 * kind + 24 * d:48 * kind + 24 * d + 24], m, r, start=True, stop=True)
            mm.then_inc(s["step_pe"], 1)

        def mask(i):
            return pb_[:, i * P:(i + 1) * P]

        def masks(i):
            return pb_[:, i * P:(i + 2) * P].rearrange("p (d t) -> p d t", d=2).unsqueeze(2).to_broadcast([P, 2, 4, P])

        flat = scr[:, :, :].rearrange("p a t -> p (a t)")
        bufs = [arena[:, 1024 * i:1024 * (i + 1)] for i in range(6)]
        bufs += [arena[:, A_V + 1024 * i:A_V + 1024 * (i + 1)] for i in range(2)]
        bufs += [flat[:, 1024 * i:1024 * (i + 1)] for i in range(4)]
        (NT, AQ, LAM_KE, LAB_B, DEC_B, QG, Y, X, XT, KT, VT, ST) = bufs
        oacc = arena[:, A_V + 2048:A_V + 2048 + 4 * T].rearrange("p (h t) -> p h t", h=4)
        PE_MARKS = ["kk", "kq", "kt", "vt", "decay", "row", "y0"] + [f"{a}{l}" for l in range(1, 7) for a in "yx"] + \
            ["wt", "u", "o", "ds"]
        ACT_MARKS = ["kk", "kt", "vt", "decay", "row"] + [f"y{l}" for l in range(1, 7)] + ["u"]
        DVE_MARKS = ["kq", "aq", "nt", "xt0", "x0"] + [f"x{l}" for l in range(1, 7)] + ["qg", "wt", "o", "s"]
        POOL_MARKS = ["lam", "lab"] + [f"b{l}" for l in range(1, 7)] + ["ke", "kg"]
        MARKS = {"pe": (PE_MARKS, 2), "act": (ACT_MARKS, 3), "dve": (DVE_MARKS, 2), "pool": (POOL_MARKS, 0)}

        def after(eng, who, st, mark):
            marks, start = MARKS[who]
            eng.wait_ge(s["step_" + who], start + len(marks) * st + marks.index(mark) + 1)

        def pair(b):
            return ps[:, b:b + 2, :].rearrange("p a t -> p (a t)")

        def sq(buf, d, hd):
            return buf[:, (4 * d + hd) * P:(4 * d + hd + 1) * P]

        def bank(b, d, hd):
            return ps[:, b + d, hd * P:(hd + 1) * P]

        EIGHT = [(d, hd) for d in range(2) for hd in range(4)]

        def chunk(tile, st, d):
            c = CH_COL[(FWD, BWD)[d][st]]
            return gd[:, tile, c:c + P]

        def pe_delta(pe, n):
            inc = lambda mm: mm.then_inc(s["step_pe"], 1)
            for st in range(6):
                if st:
                    after(pe, "act", st - 1, "u")
                for d, e in EIGHT:
                    mm = pe.matmul(bank(0, d, e), chunk(4 + e, st, d), chunk(4 + e, st, d), start=True, stop=True)
                inc(mm)
                if st:
                    after(pe, "dve", st - 1, "o")
                for d, e in EIGHT:
                    mm = pe.matmul(bank(2, d, e), chunk(4 + e, st, d), chunk(e, st, d), start=True, stop=True)
                inc(mm)
                if st:
                    after(pe, "dve", st - 1, "s")
                for d, e in EIGHT:
                    mm = pe.transpose(bank(4, d, e), chunk(4 + e, st, d), ident)
                inc(mm)
                for d, e in EIGHT:
                    mm = pe.transpose(bank(6, d, e), chunk(8 + e, st, d), ident)
                inc(mm)
                after(pe, "act", st, "kk")
                after(pe, "pool", st, "lam")
                for d, e in EIGHT:
                    mm = pe.matmul(bank(0, d, e), sq(LAM_KE, d, e), mask(2 + d), start=True, stop=True)
                inc(mm)
                after(pe, "dve", st, "kq")
                after(pe, "pool", st, "lab")
                for d, e in EIGHT:
                    mm = pe.matmul(bank(2, d, e), sq(LAB_B, d, e), mask(2 + d), start=True, stop=True)
                inc(mm)
                after(pe, "act", st, "decay")
                after(pe, "dve", st, "xt0")
                for d, e in EIGHT:
                    mm = pe.transpose(bank(0, d, e), sq(LAB_B, d, e), ident)
                inc(mm)
                for l in range(1, 7):
                    after(pe, "dve", st, f"x{l - 1}")
                    after(pe, "pool", st, f"b{l}")
                    if l == 1:
                        after(pe, "act", st, "row")
                    for d, e in EIGHT:
                        mm = pe.matmul(bank(2, d, e), sq(DEC_B if l % 2 else LAB_B, d, e), sq(X, d, e), start=True, stop=True)
                    inc(mm)
                    after(pe, "act", st, f"y{l}")
                    if l == 1:
                        after(pe, "act", st, "kt")
                    for d, e in EIGHT:
                        mm = pe.matmul(bank(0, d, e), sq(Y, d, e), sq(XT, d, e), start=True, stop=True)
                    if l < 6:
                        for d, e in EIGHT:
                            mm = pe.matmul(bank(4, d, e), sq(XT, d, e), sq(Y, d, e), start=True, stop=True)
                    inc(mm)
                after(pe, "dve", st, "x6")
                after(pe, "pool", st, "ke")
                after(pe, "act", st, "vt")
                for d, e in EIGHT:
                    mm = pe.matmul(bank(6, d, e), sq(LAM_KE, d, e), sq(XT, d, e), start=True, stop=True)
                inc(mm)
                after(pe, "dve", st, "wt")
                for d, e in EIGHT:
                    pe.matmul(bank(0, d, e), sq(XT, d, e), sq(VT, d, e), start=True, stop=False)
                    mm = pe.matmul(bank(0, d, e), sq(Y, d, e), sq(ST, d, e), start=False, stop=True)
                inc(mm)
                after(pe, "act", st, "u")
                for d, e in EIGHT:
                    pe.matmul(bank(2, d, e), sq(ST, d, e), sq(QG, d, e), start=True, stop=False)
                    mm = pe.matmul(bank(2, d, e), sq(X, d, e), sq(AQ, d, e), start=False, stop=True)
                inc(mm)
                after(pe, "pool", st, "kg")
                for d, e in EIGHT:
                    mm = pe.matmul(bank(4, d, e), sq(KT, d, e), sq(X, d, e), start=True, stop=True)
                inc(mm)

        def act_delta(act, n):
            for st in range(6):
                def take(mark, dst, b, f=ACT.Copy):
                    after(act, "pe", st, mark)
                    act.activation(dst, pair(b), f).then_inc(s["step_act"], 1)
                take("kk", NT, 0)
                take("kt", KT, 4)
                take("vt", VT, 6)
                take("decay", DEC_B, 0, ACT.Exp)
                take("row", QG, 2, ACT.Exp)
                for l in range(1, 7):
                    take(f"y{l}", Y, 2)
                take("u", X, 0)

        def dve_delta(dve, n):
            inc = lambda ins: ins.then_inc(s["step_dve"], 1)
            quad = lambda b: b.rearrange("p (d h t) -> p d h t", d=2, h=4)
            eight = lambda b: b.rearrange("p (e t) -> p e t", e=8)
            eye = ident.unsqueeze(1).to_broadcast([P, 8, P])
            dve.memset(ST, 0.0)
            dve.memset(oacc, 0.0)
            for st in range(6):
                after(dve, "pe", st, "kq")
                inc(dve.tensor_copy(AQ, pair(2)))
                after(dve, "act", st, "decay")
                dve_link(dve, n, dve.tensor_tensor(eight(DEC_B), eight(DEC_B), step_bc(beta, st), ALU.mult))
                dve_link(dve, n, dve.tensor_tensor(quad(DEC_B), quad(DEC_B), masks(2), ALU.mult))
                inc(dve.tensor_tensor(AQ, AQ, DEC_B, ALU.mult))
                inc(dve.tensor_tensor(NT, NT, DEC_B, ALU.mult))
                after(dve, "dve", st, "nt")
                after(dve, "pe", st, "row")
                dve_link(dve, n, dve.tensor_tensor(quad(LAB_B), quad(NT), masks(4), ALU.mult))
                inc(dve.scalar_tensor_tensor(eight(XT), eight(LAB_B), -1.0, eye, ALU.mult, ALU.add))
                after(dve, "pe", st, "y0")
                inc(dve.scalar_tensor_tensor(eight(X), eight(pair(0)), -1.0, eye, ALU.mult, ALU.add))
                for l in range(1, 7):
                    after(dve, "pe", st, f"x{l}")
                    after(dve, "dve", st, f"x{l - 1}")
                    ins = dve.tensor_tensor(XT, XT, pair(0), ALU.subtract)
                    if l < 6:
                        ins = dve.tensor_tensor(X, X, pair(4), ALU.subtract)
                    inc(ins)
                after(dve, "act", st, "row")
                for d in range(2):
                    c = CH_COL[(FWD, BWD)[d][st]]
                    ins = dve.tensor_tensor(quad(QG)[:, d], quad(QG)[:, d], gd[:, 0:4, c:c + P], ALU.mult)
                inc(ins)
                after(dve, "pe", st, "wt")
                inc(dve.tensor_scalar(Y, pair(6), -1.0, None, ALU.mult))
                after(dve, "pe", st, "o")
                for d in range(2):
                    c = (FWD, BWD)[d][st] * P
                    o = oacc[:, :, c:c + P]
                    dve_link(dve, n, dve.tensor_tensor(o, o, ps[:, 2 + d, :].rearrange("p (h t) -> p h t", h=4), ALU.add))
                dve.tensor_copy(small[:, 30:31], small[:, 32:33]).then_inc(s["step_dve"], 1)
                dve_link(dve, n, dve.tensor_tensor(eight(ST), eight(ST), step_bc(gates[:, 4], st), ALU.mult))
                after(dve, "pe", st, "ds")
                ins = dve.tensor_tensor(ST, ST, pair(4), ALU.add)
                inc(ins)
                after(dve, "dve", st, "s")

        def pool_delta(pool, n):
            quad = lambda b: b.rearrange("p (d h t) -> p d h t", d=2, h=4)
            eight = lambda b: b.rearrange("p (e t) -> p e t", e=8)
            inc = lambda ins: ins.then_inc(s["step_pool"], 1)
            for st in range(6):
                a = step_bc(la, st)
                if st:
                    after(pool, "pe", st - 1, "wt")
                inc(pool.tensor_tensor(quad(LAM_KE), masks(0), a.rearrange("p (d h) t -> p d h t", d=2), ALU.mult))
                if st:
                    after(pool, "pe", st - 1, "y6")
                inc(pool.tensor_copy(eight(LAB_B), a))
                for l in range(1, 7):
                    if l == 1:
                        after(pool, "dve", st, "nt")
                    elif l == 2:
                        after(pool, "pe", st, "y0")
                    else:
                        after(pool, "pe", st, f"y{l - 2}")
                    inc(pool.tensor_tensor(quad(DEC_B if l % 2 else LAB_B), quad(NT), masks(4 + 2 * l), ALU.mult))
                after(pool, "act", st, "kt")
                after(pool, "pe", st, "decay")
                inc(pool.tensor_tensor(eight(LAM_KE), eight(KT), step_bc(gates[:, 2], st), ALU.mult))
                after(pool, "pool", st, "ke")
                inc(pool.tensor_tensor(eight(KT), eight(KT), step_bc(kscale, st), ALU.mult))

        def act_silu_gate(act, n, pairs):
            for i, (g, o) in enumerate(pairs):
                act.activation(g, g, ACT.Silu).then_inc(s["gate_ready"], 1)

        def dve_silu_gate(dve, n, pairs):
            for i, (g, o) in enumerate(pairs):
                dve.wait_ge(s["gate_ready"], n.at("gate_ready") + i + 1)
                for a, b in (zip((g[:, 0:CTX], g[:, CTX + 2:GN]), o) if isinstance(o, list) else ((g, o),)):
                    dve.tensor_tensor(b, b, a, ALU.mult)

        bt = arena[:, A_BT:A_BT + 120 * 64].rearrange("p (s c) -> p s c", c=64)

        def pe_bias(pe, n):
            pe.wait_ge(s["rpb_landed"], 16)
            for g in range(16):
                if g >= 8:
                    pe.wait_ge(s["bt_read"], g - 7)
                for q in range(4):
                    c = 4 * g + q
                    mm = pe.matmul(ps[0:64, g % 8, 120 * q:120 * q + 120], band[0:31, 63 - c:127 - c], pa[0:31, 0:120],
                                   start=True, stop=True)
                mm.then_inc(s["bt_ready"], 1)

        def dve_bias(dve, n):
            dve.memset(bt[64:128, 0:1, :], 0.0)
            for g in range(16):
                dve.wait_ge(s["bt_ready"], g + 1)
                src = ps[0:64, g % 8, 0:480].rearrange("p (c s) -> p s c", c=4)
                dve.tensor_copy(bt[0:64, :, 4 * g:4 * g + 4], src)
                dve_ins = dve.tensor_copy(bt[64:128, 1:120, 4 * g:4 * g + 4], src[:, 0:119, :])
                dve_ins.then_inc(s["bt_read"], 1)
            dve.wait_ge(s["bt_read"], 16)
            dve.tensor_tensor(bt, bt, cmask.unsqueeze(1).to_broadcast([P, 120, 64]), ALU.add)

        def cut(a, m, w):
            return arena[:, a:a + m * w].rearrange("p (m t) -> p m t", m=m)

        fq = cut(0, 8, T2)
        r3 = cut(8 * T2, 12, T2)
        fv = cut(20 * T2, 5, 512)
        rv = cut(20 * T2 + 2560, 5, 512)
        ncb = cut(20 * T2 + 5120, 8, T2)
        ro = cut(28 * T2 + 5120, 4, T2)
        rs0 = 32 * T2 + 5120
        rbuf = [arena[:, rs0 + 512 * i:rs0 + 512 * (i + 1)] for i in range(4)]
        HALF = T2 // 2

        cum = scr[0:8, 2, 0:T2]
        FTILES = [(META + P * t, P) for t in range(4)] + [(0, META)]

        def pe_forget(pe, n, l):
            b = n.at("forget")
            pe.wait_ge(s["small_landed"], 32 + 16 * l)
            for q in range(2):
                for k in range(KD):
                    mm = pe.matmul(ps[0:8, q, 0:HALF], wsmall[:, k, 0:8], h[:, k, TOK2 + q * HALF:TOK2 + (q + 1) * HALF],
                                   start=(k == 0), stop=(k == KD - 1))
            mm.then_inc(s["f_logits"], 1)
            pe.wait_ge(s["f_cum"], b + 1)
            for t, (c0, rows) in enumerate(FTILES):
                mm = pe.matmul(ps[0:rows, 2, 8 * t:8 * t + 8], cum[:, c0:c0 + rows], ident[0:8, 0:8], start=True, stop=True)
            mm.then_inc(s["f_logits"], 1)
            for e in range(8):
                if e >= 2:
                    pe.wait_ge(s["f_read"], 8 * b + e - 1)
                for q in range(2):
                    mm = pe.matmul(ps[:, 4 + 2 * (e % 2) + q, 0:HALF], pb_[0:8, 1024 + e * P:1024 + (e + 1) * P],
                                   cum[:, q * HALF:(q + 1) * HALF], start=True, stop=True)
                mm.then_inc(s["f_rows"], 1)

        def act_forget(act, n, l):
            b = n.at("forget")
            act.wait_ge(s["f_z"], b + 1)
            z, t = scr[0:8, 3, 0:T2], scr[0:8, 4, 0:T2]
            act_link(act, n, act.activation(t, z, ACT.Abs))
            act_link(act, n, act.activation(t, t, ACT.Exp, scale=-1.0))
            act.activation(t, t, ACT.Ln, bias=1.0).then_inc(s["f_log"], 1)
            for e in range(8):
                act.wait_ge(s["f_rows"], 8 * b + e + 1)
                act.copy(ncb[:, e, :].rearrange("p (a t) -> p a t", a=2), ps[:, 4 + 2 * (e % 2):6 + 2 * (e % 2), 0:HALF]
                         ).then_inc(s["f_read"], 1)

        def dve_forget(dve, n, l):
            b = n.at("forget")
            z, t = scr[0:8, 3, 0:T2], scr[0:8, 4, 0:T2]
            dve.memset(scr[0:8, 5, 0:T2], 1.0)
            dve.wait_ge(s["f_logits"], 2 * b + 1)
            dve.tensor_scalar(z.rearrange("p (a t) -> p a t", a=2), ps[0:8, 0:2, 0:HALF], vec[0:8, VEC["b_fgate"] + l:VEC["b_fgate"] + l + 1],
                              None, ALU.add).then_inc(s["f_z"], 1)
            dve.wait_ge(s["f_log"], b + 1)
            dve_link(dve, n, dve.scalar_tensor_tensor(z, z, 0.0, t, ALU.min, ALU.subtract))
            dve.tensor_tensor_scan(cum, scr[0:8, 5, 0:T2], z, 0.0, ALU.mult, ALU.add).then_inc(s["f_cum"], 1)
            dve.wait_ge(s["f_logits"], 2 * b + 2)
            dve.tensor_copy(small[:, 32:64], ps[:, 2, 0:32])
            dve.tensor_copy(small[0:META, 64:72], ps[0:META, 2, 32:40])

        def act_rotate(act, n, l):
            for i in range(8):
                if i >= 2:
                    act.wait_ge(s["turned"], 8 * l + i - 1)
                act.copy(scr[0:64, i % 2, 0:T2], r3[64:128, i, :])
                act.copy(scr[64:128, i % 2, 0:T2], r3[0:64, i, :]).then_inc(s["swapped"], 1)

        def dve_rotate(dve, n, l):
            for i in range(8):
                k = 1.0 if i < 4 else 128 ** -0.5
                dve_link(dve, n, dve.scalar_tensor_tensor(scr[:, 2 + i % 2, 0:T2], r3[:, i, :], k, pa[:, 0:T2], ALU.mult, ALU.mult))
                dve.wait_ge(s["swapped"], 8 * l + i + 1)
                dve_link(dve, n, dve.scalar_tensor_tensor(scr[:, i % 2, 0:T2], scr[:, i % 2, 0:T2], k, pa[:, T2:2 * T2],
                                                          ALU.mult, ALU.mult))
                dve.tensor_tensor(r3[:, i, :], scr[:, i % 2, 0:T2], scr[:, 2 + i % 2, 0:T2], ALU.add).then_inc(s["turned"], 1)

        CHUNKS = [(0, META, 4)] + [(META + P * c, P, c) for c in range(4)]
        AR, KR, QR, SR = rbuf

        def heads4(buf, rows, cols):
            return buf.rearrange("p (h t) -> p h t", h=4)[0:rows, :, 0:cols]

        def pe_retention(pe, n, l):
            for i, (c0, rows, vt) in enumerate(CHUNKS):
                at = 5 * l + i
                if at:
                    pe.wait_ge(s["r_out"], at)
                for e in range(4):
                    pe.matmul(ps[0:rows, 0, e * P:e * P + rows], r3[:, 4 + e, c0:c0 + rows], r3[:, e, c0:c0 + rows], start=True, stop=True)
                for e in range(4):
                    mm = pe.transpose(ps[0:rows, 1, e * P:e * P + P], r3[:, 4 + e, c0:c0 + rows], ident)
                mm.then_inc(s["r_raw"], 1)
                pe.wait_ge(s["r_scaled"], at + 1)
                for e in range(4):
                    vv = rv[0:rows, vt, e * P:(e + 1) * P]
                    mm = pe.matmul(ps[:, 2, e * P:e * P + rows], vv, heads4(AR, rows, rows)[:, e], start=True, stop=(i == 0))
                    if i:
                        pe.matmul(ps[:, 2, e * P:e * P + rows], heads4(SR, P, P)[:, e], heads4(QR, P, P)[:, e], start=False, stop=True)
                for e in range(4):
                    mm = pe.matmul(ps[:, 3, e * P:(e + 1) * P], heads4(KR, rows, P)[:, e], rv[0:rows, vt, e * P:(e + 1) * P],
                                   start=True, stop=True)
                mm.then_inc(s["r_sums"], 1)

        def dve_retention(dve, n, l):
            dec = pb_[:, 0:512].rearrange("p (h t) -> p h t", h=4)
            qd = pb_[:, 512:1024].rearrange("p (h t) -> p h t", h=4)
            for i, (c0, rows, vt) in enumerate(CHUNKS):
                at = 5 * l + i
                kd = pb_[0:rows, 2048 + (4 if i == 0 else 0):2048 + (8 if i == 0 else 4)]
                dve.wait_ge(s["r_raw"], at + 1)
                if i:
                    dve.tensor_tensor(heads4(QR, P, P), r3[:, 0:4, c0:c0 + P], qd, ALU.mult)
                dve.tensor_tensor(heads4(AR, rows, rows), ps[0:rows, 0, :].rearrange("p (h t) -> p h t", h=4)[:, :, 0:rows],
                                  dec[0:rows, :, 0:rows], ALU.mult)
                dve.tensor_tensor(heads4(KR, rows, P), ps[0:rows, 1, :].rearrange("p (h t) -> p h t", h=4),
                                  kd.unsqueeze(2).to_broadcast([rows, 4, P]), ALU.mult).then_inc(s["r_scaled"], 1)
                dve.wait_ge(s["r_sums"], at + 1)
                dve.tensor_copy(ro[:, :, c0:c0 + rows], ps[:, 2, :].rearrange("p (h t) -> p h t", h=4)[:, :, 0:rows])
                if i:
                    dve_link(dve, n, dve.tensor_tensor(heads4(SR, P, P), heads4(SR, P, P), qd[:, :, P - 1:P].to_broadcast([P, 4, P]),
                                                       ALU.mult))
                    dve_link(dve, n, dve.tensor_tensor(SR, SR, ps[:, 3, :], ALU.add))
                else:
                    dve_link(dve, n, dve.tensor_copy(SR, ps[:, 3, :]))
                dve.tensor_copy(small[:, 30:31], small[:, 29:30]).then_inc(s["r_out"], 1)

        def pe_centre(pe, n, l):
            for e in range(4):
                for q in range(2):
                    mm = pe.matmul(ps[:, 2 * e + q, 0:HALF], ones, ro[:, e, q * HALF:(q + 1) * HALF], start=True, stop=True)
                mm.then_inc(s["means"], 1)

        def dve_centre(dve, n, l):
            for e in range(4):
                dve.wait_ge(s["means"], 4 * l + e + 1)
                y = ro[:, e, :].rearrange("p (a t) -> p a t", a=2)
                dve.scalar_tensor_tensor(y, ps[:, 2 * e:2 * e + 2, 0:HALF], -1.0 / P, y, ALU.mult, ALU.add)

        def pe_final(pe, n):
            for t in range(4):
                for k in range(KD):
                    mm = pe.transpose(ps[:, 2 * t + k // 4, (k % 4) * P:(k % 4 + 1) * P], h[:, k, CTX + t * P:CTX + (t + 1) * P], ident)
                mm.then_inc(s["final_ready"], 1)

        def dve_final(dve, n):
            for t in range(4):
                dve.wait_ge(s["final_ready"], t + 1)
                dve.tensor_copy(arena[:, t * D:(t + 1) * D], ps[:, 2 * t:2 * t + 2, :].rearrange("p a t -> p (a t)")
                                ).then_inc(s["out_ready"], 1)

        qk = arena[:, 0:8 * T].rearrange("p (m t) -> p m t", m=8)
        v0 = arena[:, A_V:A_V + 6 * 512].rearrange("p (t f) -> p t f", t=6)
        q1 = arena[:, A_Q1:A_Q1 + 8 * LAT].rearrange("p (m t) -> p m t", m=8)
        k1 = arena[:, A_K1:A_K1 + 8 * T].rearrange("p (m t) -> p m t", m=8)
        v1 = arena[:, A_V1:A_V1 + 6 * 1024].rearrange("p (t f) -> p t f", t=6)
        TILES = [(c * P, P) for c in range(NCH)]

        def diff_units():
            units = []
            for e in range(4):
                for t in range(NCH):
                    nk = CTX if t < 2 else T
                    units.append(dict(nq=P, nk=nk, q=[qk[64 * m:64 * m + 64, e, t * P:(t + 1) * P] for m in range(2)],
                                      k=[qk[64 * m:64 * m + 64, 4 + e, :] for m in range(2)],
                                      segs=[(0, 0, nk // 2), (1, nk // 2, nk // 2)], keys=[(c * P, P) for c in range(nk // P)],
                                      v=[v0[:, c, e * P:(e + 1) * P] for c in range(nk // P)], o_part=(0, P),
                                      p=2 + len(units) % 2, out=mix[:, e, t * P:(t + 1) * P]))
            return units

        def near_units():
            units = []
            for e in range(8):
                for t in range(4):
                    j0 = 15 * e + 7 - 2 * t
                    table = bt[:, j0:j0 + 8, :].rearrange("p s c -> p (s c)")
                    units.append(dict(nq=P, nk=T, q=[q1[:, e, t * P:(t + 1) * P]], k=[k1[:, e, :]],
                                      segs=[(0, 0, CTX), (1, CTX, LAT)], keys=[(c * P, P) for c in range(6)],
                                      bias=[("plain", None), ("table", table)], diag=None,
                                      v=[v1[:, c, e * P:(e + 1) * P] for c in range(6)], o_part=(0, P),
                                      p=len(units) % 2, out=mix[:, e, CTX + t * P:CTX + (t + 1) * P]))
            return units

        def fox_units():
            units = []
            for e in range(8):
                r0 = 64 * (e % 2)
                for t in range(-1, 4):
                    c0, nq = (0, META) if t < 0 else (META + P * t, P)
                    nk = c0 + nq
                    segs = [(0, 0, nk)] if nk <= 512 else [(0, 0, nk // 2), (1, nk // 2, nk // 2)]
                    ct = 32 + 8 * (4 if t < 0 else t) + e
                    arg = ("decay", (small[0:nq, ct:ct + 1], ncb[0:nq, e, :]))
                    units.append(dict(nq=nq, nk=nk, q=[fq[r0:r0 + 64, e // 2, c0:c0 + nq]], k=[fq[r0:r0 + 64, 4 + e // 2, :]],
                                      segs=segs, bias=[arg, arg], diag=c0,
                                      keys=[(META + P * c, P) for c in range(t + 1)] + [(0, META)],
                                      v=[fv[:, c, 64 * e:64 * e + 64] for c in range(t + 1)] + [fv[0:META, 4, 64 * e:64 * e + 64]],
                                      o_part=(r0, 64), p=len(units) % 2,
                                      out=mix[r0:r0 + 64, e // 2, TOK2 + c0:TOK2 + c0 + nq]))
            return units

        def walk(eng, n, f):
            def stage(name, counts, *args):
                if name in f:
                    f[name](eng, n, *args)
                for key, k in counts.items():
                    n.add(key, k)

            def project(halves, turns, dst, acts=h, scale=None):
                stage("project", {}, acts, halves, turns)
                stage("copy_out", dict(turn=turns, tile_read=4 * turns, block_done=4 * turns), halves, turns, dst, scale)

            def project_tok(tiles, turns, dst):
                stage("project_tok", {}, h, tiles, turns)
                stage("copy_tok", dict(turn=turns, tile_read=4 * turns, block_done=4 * turns), tiles, turns, dst)

            def out_proj(halves, gate):
                stage("project", {}, mix, halves, 2)
                stage("residual", dict(turn=2, tile_read=8, block_done=8), halves, 2, gate, False)
                end_phase(eng, n)

            def feed_forward(halves, gate):
                stage("project", {}, h, halves, 11)
                stage("gates", {}, halves)
                stage("products", dict(turn=11, tile_read=44, block_done=44, gate_ready=22), halves)
                end_phase(eng, n)
                stage("down", {}, halves)
                stage("residual", dict(turn=4, tile_read=8, block_done=16), halves, 4, gate, True)
                end_phase(eng, n)

            def norm(halves, a=None, shift=None, gain=None):
                stage("norm", dict(squares_ready=8, squares_used=8, roots_ready=1, scaled_ready=8 if gain is None else 0,
                                   modulated=8 if gain is None else 0), *((halves, a, shift, gain)))
                end_phase(eng, n)

            def head_norm(tiles, matrix, scale, rope=False):
                t = len(tiles)
                stage("head_norm", dict(squares_ready=t, sums_ready=t, roots_ready=t, head_scaled=t), tiles, matrix, scale, rope)
                end_phase(eng, n)

            def attend(units, maps, bias):
                u = len(units)
                stage("attend", dict(scores_ready=u * maps, bias_ready=u * maps, exp_done=u * maps, p_ready=u, pt_psum=u,
                                     pt_copied=u, pv_done=u, o_read=u), units, maps, bias)
                end_phase(eng, n)

            stage("setup", dict(act_chain=0))
            stage("ada", dict(turn=24, tile_read=96, block_done=96))
            end_phase(eng, n)

            norm(BOTH, 0, 0)
            project(BOTH, 2, lambda m, b: qk[:, m, BOTH[b][0]:BOTH[b][0] + BOTH[b][1]])
            project(BOTH, 4, lambda m, b: gd[:, m, (2, 260)[b]:(2, 260)[b] + BOTH[b][1]])
            project_tok(TILES, 1, v0)
            end_phase(eng, n)
            stage("tables1", {})
            stage("gates_raw", {})
            end_phase(eng, n)
            head_norm([(qk[:, m, :], qk[:, m, :], v("diff_gain", m // 4), T) for m in range(8)], bo64, 1.0 / 64, rope=True)
            attend(diff_units(), 2, False)
            head_norm([(mix[:, m, :], mix[:, m, :], v("subln"), T) for m in range(4)], ones, 1.0 / P)
            stage("conv", {})
            end_phase(eng, n)
            head_norm([(gd[:, m, 2:2 + GN], gd[:, m, 2:2 + GN], P ** -0.5 if m < 4 else 1.0, GN) for m in range(8)], ones, 1.0)
            stage("gates_tab", {})
            end_phase(eng, n)
            stage("delta", {})
            end_phase(eng, n)
            head_norm([(oacc[:, e, :], mix[:, 4 + e, :], v("gdn_norm"), T) for e in range(4)], ones, 1.0 / P)
            stage("silu_gate", dict(gate_ready=4),
                  [(gd[:, 12 + e, 2:2 + GN], [mix[:, 4 + e, 0:CTX], mix[:, 4 + e, CTX:T]]) for e in range(4)])
            end_phase(eng, n)
            out_proj(BOTH, 16)
            norm(BOTH, 1, 24)
            feed_forward(BOTH, 40)
            stage("load_rpb", {})
            norm(BOTH, 2, 48)
            project(LATENT, 2, lambda m, b: q1[:, m, :])
            project(BOTH, 2, lambda m, b: k1[:, m, BOTH[b][0]:BOTH[b][0] + BOTH[b][1]])
            project_tok(TILES, 2, v1)
            end_phase(eng, n)
            stage("bias", {})
            end_phase(eng, n)
            head_norm([(q1[:, m, :], q1[:, m, :], v("na_gain", 0), LAT) for m in range(8)]
                      + [(k1[:, m, :], k1[:, m, :], v("na_gain", 1), T) for m in range(8)], ones, 1.0 / P)
            attend(near_units(), 1, True)
            stage("load_second", {})
            out_proj(LATENT, 48 + 16)
            norm(LATENT, 3, 48 + 24)
            feed_forward(LATENT, 48 + 40)
            stage("tables2", {})
            for l in range(2):
                norm(SECOND, gain=lambda k, l=l: v("attn_norm", 8 * l + k))
                cols = lambda b: slice(b * HALF, (b + 1) * HALF)
                project(SECOND, 1, lambda m, b: fq[:, m, cols(b)], scale=0.125)
                project(SECOND, 1, lambda m, b: fq[:, 4 + m, cols(b)])
                project(SECOND, 3, lambda m, b: r3[:, m, cols(b)])
                tiles2 = [(TOK2 + c0, rows) for c0, rows in FTILES]
                project_tok(tiles2, 1, fv)
                project_tok(tiles2, 1, rv)
                end_phase(eng, n)
                stage("forget", dict(forget=1), l)
                end_phase(eng, n)
                if l == 0:
                    stage("load_forget", {})
                attend(fox_units(), 1, True)
                stage("rotate", {}, l)
                end_phase(eng, n)
                stage("retention", {}, l)
                end_phase(eng, n)
                stage("centre", {}, l)
                end_phase(eng, n)
                head_norm([(ro[:, e, :], mix[:, 4 + e, TOK2:T], v("ret_gn", 4 * l + e), T2) for e in range(4)], ones, 1.0 / P)
                stage("silu_gate", dict(gate_ready=4), [(r3[:, 8 + e, :], mix[:, 4 + e, TOK2:T]) for e in range(4)])
                end_phase(eng, n)
                out_proj(SECOND, None)
                norm(SECOND, gain=lambda k, l=l: v("ffn_norm2", 8 * l + k))
                feed_forward(SECOND, None)
            norm(SECOND, gain=lambda k: v("final", k))
            stage("final", {})

        @block.tensor
        def _(pe):
            walk(pe, Tally(), dict(
                ada=pe_ada, project=pe_project, project_tok=pe_project_tok, down=pe_down,
                norm=lambda pe, n, hv, a, sh, g: pe_norm(pe, n, hv), head_norm=pe_head_norm, attend=pe_attend,
                gates_raw=pe_gates_raw, gates_tab=pe_gates_tab, delta=pe_delta, bias=pe_bias, forget=pe_forget,
                retention=pe_retention, centre=pe_centre, final=pe_final))

        @block.scalar
        def _(act):
            walk(act, Tally(), dict(
                setup=act_setup, norm=lambda act, n, hv, a, sh, g: act_norm(act, n, hv, a, sh), gates=act_gates,
                head_norm=act_head_norm, attend=act_attend, conv=act_conv, gates_tab=act_gates_tab, delta=act_delta,
                silu_gate=act_silu_gate, forget=act_forget, rotate=act_rotate))

        @block.vector
        def _(dve):
            walk(dve, Tally(), dict(
                setup=dve_setup, ada=dve_ada, copy_out=dve_copy_out, copy_tok=dve_copy_tok, residual=dve_residual,
                products=dve_products, norm=lambda dve, n, hv, a, sh, g: dve_norm(dve, n, hv, g), head_norm=dve_head_norm,
                attend=dve_attend, conv=dve_conv, gates_raw=dve_gates_raw, gates_tab=dve_gates, delta=dve_delta,
                silu_gate=dve_silu_gate, bias=dve_bias, forget=dve_forget, rotate=dve_rotate, retention=dve_retention,
                centre=dve_centre, final=dve_final, tables1=lambda dve, n: dve.wait_ge(s["tables_landed"], 32)))

        @block.gpsimd
        def _(pool):
            def tables(pool, a, b):
                pool.dma_start(pa[:, :], dram[a]).then_inc(s["tables_landed"], 16)
                pool.dma_start(pb_[:, :], dram[b]).then_inc(s["tables_landed"], 16)

            def first(pool, n):
                tables(pool, "rope1", "masks")
                pool.dma_start(wsmall[:, :, :], dram["gate_w"]).then_inc(s["small_landed"], 16)

            def load_rpb(pool, n):
                pool.dma_start(pa[0:31, 0:120], dram["rpbT"]).then_inc(s["rpb_landed"], 16)

            def load_second(pool, n):
                tables(pool, "rope2", "ret")
                pool.dma_start(wsmall[:, :, 0:8], dram["forget_w0"]).then_inc(s["small_landed"], 16)
                pool.dma_start(x[:, :, TOK2:CTX], dram["metaT"]).then_inc(s["meta_landed"], 16)
                pool.wait_ge(s["meta_landed"], 16)
                pool.wait_ge(s["tables_landed"], 64)

            def load_forget(pool, n):
                pool.dma_start(wsmall[:, :, 0:8], dram["forget_w1"]).then_inc(s["small_landed"], 16)

            walk(pool, Tally(), dict(setup=first, delta=pool_delta, load_rpb=load_rpb, load_second=load_second,
                                     load_forget=load_forget))


def kernel(**inputs):
    import concourse.bacc as bacc
    from concourse.bass_utils import run_bass_kernel_spmd as run

    a = {k: np.asarray(z) for k, z in inputs.items()}

    def blocks(w):
        k, m = w.shape
        return w.reshape(k // P, P, m // P, P).transpose(2, 1, 0, 3).reshape(m // P, P, k)

    def down(w):
        b = blocks(w).reshape(KD, P, 2, SLOT_K * P)
        return b.transpose(0, 2, 1, 3).reshape(2 * KD, P, SLOT_K * P)

    def gate_up(g, u):
        return np.stack([blocks(g), blocks(u)], 1).reshape(2 * FK, P, D)

    def cols(z):
        return z.reshape(-1, P).T

    def kp(z):
        return z.reshape(-1, P, z.shape[-1]).transpose(1, 0, 2)

    ew, ow = a["even_w_in"][0], a["odd_w_in"][0]
    maps = {
        "xT": kp(a["x"][0].T), "ctxT": kp(a["ctx"][0].T), "metaT": kp(a["meta_tokens_2"].T),
        "ada": np.concatenate([blocks(a["ada_w"][l]) for l in range(2)]),
        "even_in": np.concatenate([blocks(ew[:, 0:1024]), blocks(ew[:, 1536:3072]), blocks(ew[:, 3072:3584]),
                                   blocks(ew[:, 1024:1536])]),
        "gate_w": kp(ew[:, 3584:3600]), "even_out": blocks(a["even_w_out"][0]),
        "odd_in": blocks(ow), "odd_out": blocks(a["odd_w_out"][0]), "rpbT": a["na_rpb"][0].reshape(120, 31).T,
    }
    for l in range(2):
        f = a["ffn_w_in"][l]
        maps[f"gu{l}"] = gate_up(f[:, :FF], f[:, FF:])
        maps[f"dn{l}"] = down(a["ffn_w_out"][l])
        w = a["w_in_2"][l]
        maps[f"in2_{l}"] = np.concatenate([blocks(w[:, lo:lo + 512]) for lo in (0, 512, 1544, 2056, 3080, 1024, 2568)])
        maps[f"forget_w{l}"] = kp(w[:, 1536:1544])
        maps[f"out2_{l}"] = blocks(a["w_out_2"][l])
        maps[f"gu2_{l}"] = gate_up(a["w_gate_2"][l], a["w_up_2"][l])
        maps[f"dn2_{l}"] = down(a["w_down_2"][l])

    def row(z):
        return np.broadcast_to(z.reshape(1, -1), (P, z.size))

    bf = np.zeros((P, 2), np.float32)
    bf[0:8] = a["b_fgate_2"].T
    vecs = {"norm_mix": cols(a["norm_mix"]), "norm_ffn": cols(a["norm_ffn"]), "attn_norm": cols(a["attn_norm_2"]),
            "ffn_norm2": cols(a["ffn_norm_2"]), "final": cols(a["final_norm_2"]),
            "diff_gain": np.concatenate([a["diff_qk_gain"][0].T] * 2, 0), "subln": cols(a["diff_subln"]),
            "gdn_norm": cols(a["gdn_norm"]),
            "conv": a["gdn_conv"][0].T.reshape(12, P, 5).transpose(1, 0, 2).reshape(P, 60),
            "na_gain": a["na_qk_gain"][0].T, "ret_gn": cols(a["ret_gn_2"]), "ada_b": cols(a["ada_b"]), "b_fgate": bf,
            "c": np.stack([cols(a["c"]), cols(a["c_ctx"])], 2).reshape(P, 16),
            "dt_bias": row(a["gdn_dt_bias"]), "a_log": row(a["gdn_a_log"]), "lam": row(a["diff_lambda"])}
    maps["vecs"] = np.concatenate([vecs[k] for k in VEC], 1)
    maps.update(shape_tables())
    maps = {k: np.ascontiguousarray(z) for k, z in maps.items()}

    nc = bacc.Bacc("TRN2", target_bir_lowering=False, num_devices=1)
    dram = {k: nc.dram_tensor(f"in_{k}", z.shape, F32, kind="ExternalInput").ap() for k, z in maps.items()}
    out = nc.dram_tensor("result", (LAT, D), F32, kind="ExternalOutput").ap()
    build(nc, dram, out)
    r = run(nc, [{f"in_{k}": z for k, z in maps.items()}], core_ids=[0])
    return r.results[0]["result"].reshape(1, LAT, D)
```

```python
import math
from contextlib import ExitStack

import concourse.bass as bass
from concourse import mybir
import numpy as np

F32 = mybir.dt.float32
F32R = mybir.dt.float32r
ACT = mybir.ActivationFunctionType
ALU = mybir.AluOpType
AX = mybir.AxisListType

P = 128
D = 1024
KD = D // P
CTX, LAT, META = 256, 512, 16
T = CTX + LAT
TOK2 = CTX - META
T2 = META + LAT
EPS = 1e-6
FF = 2816
FK = FF // P
SLOTS = 2
SLOT_K = 11
BOTH = [(0, CTX), (CTX, LAT)]
LATENT = [(CTX, LAT)]
SECOND = [(TOK2, T2 // 2), (TOK2 + T2 // 2, T2 // 2)]
H4 = 4
GW = 774
NCH = T // P
CH_COL = [2, 2 + P, 260, 260 + P, 260 + 2 * P, 260 + 3 * P]
FWD = [0, 1, 2, 3, 4, 5]
BWD = [1, 0, 5, 4, 3, 2]
LEVELS = 7
RET_LOG_GAMMA = [math.log(1.0 - 2.0 ** (-5 - h)) for h in range(4)]
BIG = 1e30
FIRST_BYTE = 16512

VEC = {}
_at = 0
for _name, _n in (("norm_mix", 16), ("norm_ffn", 16), ("attn_norm", 16), ("ffn_norm2", 16), ("final", 8),
                  ("diff_gain", 2), ("subln", 1), ("gdn_norm", 1), ("conv", 60), ("na_gain", 2),
                  ("ret_gn", 8), ("ada_b", 96), ("b_fgate", 2), ("c", 16),
                  ("dt_bias", 8), ("a_log", 8), ("lam", 256)):
    VEC[_name] = _at
    _at += _n
NVEC = _at

A_QK = 0
A_GD = 8 * T
A_V = A_GD + 16 * GW
A_MASKS = A_V
A_NORM = FK * T
A_RET = 22016
A_SIZE = 23104
A_Q1, A_K1, A_V1, A_BT = 0, 8 * LAT, 8 * LAT + 8 * T, 8 * LAT + 8 * T + 6 * 8 * P
NPA = 1056
NMASK = 18 * P
NRET = 1024 + 8


class Tally(dict):

    def at(self, name):
        return self.get(name, 0)

    def add(self, name, k=1):
        self[name] = self.get(name, 0) + k
        return self[name]


def shape_tables():
    i = np.arange(P)
    r, c = i[:, None], i[None, :]
    ident = np.eye(P)
    bo64 = (r // 64 == c // 64).astype(np.float64)
    cmask = np.zeros((P, 64))
    q = i % 64
    start = np.clip(q - 8, 0, 48)
    kk = np.arange(64)[None, :]
    cmask[:] = np.where((kk >= start[:, None]) & (kk < start[:, None] + 16), 0.0, -BIG)
    band = np.zeros((P, 128))
    n = np.arange(127)
    for j in range(31):
        band[j, :127] = (78 - n == j)
    dmask = np.where(c <= r, 0.0, -BIG)
    base = np.concatenate([ident, np.ones((P, P)), bo64, cmask, band, dmask], 1)

    inv = 10000.0 ** (-np.arange(16, dtype=np.float32) / np.float32(16))
    t = np.arange(LAT)
    ang = np.concatenate([(t // 64).astype(np.float32)[:, None] * inv, (t % 64).astype(np.float32)[:, None] * inv], 1)
    f = (i % 64) // 2
    cos1 = np.cos(ang)[:, f].T
    sin1 = np.sin(ang)[:, f].T * np.where(i % 2 == 0, -1.0, 1.0)[:, None]
    rope1 = np.concatenate([cos1, sin1, np.zeros((P, NPA - 2 * LAT))], 1)
    inv2 = 10000.0 ** (-np.arange(0, 128, 2, dtype=np.float32) / np.float32(128))
    ang2 = np.arange(T2, dtype=np.float32)[:, None] * inv2[None]
    cos2 = np.cos(ang2)[:, i % 64].T
    sin2 = np.sin(ang2)[:, i % 64].T * np.where(i < 64, -1.0, 1.0)[:, None]
    rope2 = np.concatenate([cos2, sin2], 1)

    mats = [(r > c), (r < c), (r <= c), (r >= c)]
    for lv in range(LEVELS):
        same = (r >> (lv + 1)) == (c >> (lv + 1))
        rb, cb = (r >> lv) & 1, (c >> lv) & 1
        mats += [same & (rb == 0) & (cb == 1), same & (rb == 1) & (cb == 0)]
    masks = np.concatenate([m.astype(np.float64) for m in mats], 1)
    lg = np.array(RET_LOG_GAMMA)
    s, tt = r, c
    dec = [np.where(tt >= s, np.exp(np.maximum(tt - s, 0) * lg[h]), 0.0) for h in range(4)]
    qd = [np.broadcast_to(np.exp((i + 1.0) * lg[h])[None], (P, P)) for h in range(4)]
    kd = np.stack([np.exp((P - 1.0 - i) * lg[h]) for h in range(4)], 1)
    kdm = np.stack([np.exp((META - 1.0 - i) * lg[h]) * (i < META) for h in range(4)], 1)
    ret = np.concatenate(dec + qd + [kd, kdm], 1)
    out = [np.ascontiguousarray(a, np.float32) for a in (base, rope1, rope2, masks, ret)]
    return dict(zip(("base", "rope1", "rope2", "masks", "ret"), out))


def build(nc, dram, out):
    with ExitStack() as ctx:
        place = {}
        at = [FIRST_BYTE]

        def sb(name, shape, dtype=F32, over=None, skip=0):
            size = 4 * int(np.prod(shape[1:]))
            if over is None:
                offset = at[0]
                at[0] += (size + 31) // 32 * 32
            else:
                offset = place[over] + 4 * skip
            place[name] = offset
            return nc.alloc_sbuf_tensor_at(name, shape, dtype, offset=offset)

        x = sb("resid", [P, KD, T])
        mix = sb("mix", [P, KD, T])
        act_lo = sb("act_lo", [P, KD, T], F32R, "mix")
        act_hi = sb("act_hi", [P, KD, T], F32R)
        scr = sb("scr", [P, 6, GW], F32, "act_hi")
        raw = sb("raw", [P, SLOTS, SLOT_K * P])
        w_hi = sb("w_hi", [P, SLOTS, SLOT_K * P], F32R)
        w_lo = sb("w_lo", [P, SLOTS, SLOT_K * P], F32R)
        arena = sb("arena", [P, A_SIZE])
        ff_hi = sb("ff_hi", [P, SLOT_K, T], F32R, "arena")
        ff_lo = sb("ff_lo", [P, SLOT_K, T], F32R, "arena", SLOT_K * T)
        diags = sb("diags", [P, 2, 2, P], F32, "act_hi", KD * T - 4 * P)
        nscr = sb("nscr", [P, 6, GW], F32, "arena", A_NORM)
        pb_ = sb("masks", [P, NMASK], F32, "arena", A_MASKS)
        ret_tab = sb("ret_tab", [P, NRET], F32, "arena", A_RET)
        base = sb("base", [P, 3 * P + 64 + 128 + P])
        pa = sb("pa", [P, NPA])
        vec = sb("vec", [P, NVEC])
        mod = sb("mod", [P, 96, 2])
        amod = sb("amod", [P, 4, KD, 2])
        csil = sb("csil", [P, KD, 2])
        wsmall = sb("wsmall", [P, KD, 16])
        small = sb("small", [P, 96])
        gates = sb("gates", [P, 8, 48])
        eps_t = sb("eps_t", [P, 8])
        eps_ap = eps_t[:, 0:1]
        ps = ctx.enter_context(nc.psum_tensor("ps", [P, 8, 512], F32))

        names = ("inputs_landed", "tables_landed", "small_landed", "rpb_landed", "meta_landed", "block_done",
                 "tile_read", "gate_ready", "hi_ready", "lo_ready", "ada_used", "ada_rows", "ada_turned", "ada_read", "token_block", "token_tiles", "token_staged",
                 "product_step", "mix_hi", "parts_ready", "squares_ready", "squares_used",
                 "sums_ready", "roots_ready", "scaled_ready", "modulated", "head_scaled", "swapped",
                 "scores_ready", "bias_ready", "exp_done", "p_ready", "pt_psum", "pt_copied", "pv_done",
                 "o_read", "phase_done", "act_chain", "dve_chain", "pool_chain", "setup_ready", "small_hi", "small_parts", "gates_rows", "gates_staged",
                 "conv_first", "conv_ready", "conv_used", "bt_ready", "bt_read", "f_logits", "f_z", "f_log", "f_cum", "f_rows",
                 "f_read", "turned", "r_raw", "r_scaled", "r_sums", "r_out", "means", "final_ready", "step_pe", "step_act", "step_dve", "step_pool", "out_ready", "stored")
        s = {n: ctx.enter_context(nc.semaphore(n)) for n in names}
        w_landed = [ctx.enter_context(nc.semaphore(f"w_landed{i}")) for i in range(SLOTS)]
        ada_landed = [ctx.enter_context(nc.semaphore(f"ada_landed{i}")) for i in range(4)]
        ada_ring = arena[:, 0:4 * 4 * D].rearrange("p (r c) -> p r c", r=4)

        ident = base[:, 0:P]
        ones = base[:, P:2 * P]
        bo64 = base[:, 2 * P:3 * P]
        cmask = base[:, 3 * P:3 * P + 64]
        band = base[:, 3 * P + 64:3 * P + 64 + 128]
        dmask = base[:, 3 * P + 192:4 * P + 192]

        def v(name, i=0, n=1):
            return vec[:, VEC[name] + i:VEC[name] + i + n]

        def v_at(name, i):
            return vec[:, :].rearrange("p (n o) -> p n o", o=1)[:, VEC[name] + i, :]

        def bc(ap, shape):
            return ap.to_broadcast(shape)

        FULL, PART = KD * P, SLOT_K * P

        def layer(name_in, turns, name_out, ffn):
            return [(name_in, 0, turns, FULL), (name_out, 0, 4, FULL), (f"gu{ffn}", 0, 11, FULL), (f"dn{ffn}", 0, 4, PART),
                    (f"gu{ffn}", 22, 11, FULL), (f"dn{ffn}", 8, 4, PART)]

        stream = layer("even_in", 14, "even_out", "0") + layer("odd_in", 12, "odd_out", "1")
        for l in range(2):
            stream += layer(f"in2_{l}", 14, f"out2_{l}", f"2_{l}")
        ahead = [c for _, _, turns, c in stream for _ in range(turns)][1:] + [0]

        block = ctx.enter_context(nc.Block())

        def end_phase(eng, n):
            count = n.add("phase")
            if not n.at("free_running"):
                eng.drain().then_inc(s["phase_done"], 1)
                eng.wait_ge(s["phase_done"], 3 * count)

        @block.sync
        def _(sp):
            sp.dma_start(vec[:, :], dram["vecs"]).then_inc(s["inputs_landed"], 16)
            sp.dma_start(base[:, :], dram["base"]).then_inc(s["inputs_landed"], 16)
            sp.dma_start(x[:, :, 0:CTX], dram["ctxT"]).then_inc(s["inputs_landed"], 16)
            sp.dma_start(x[:, :, CTX:T], dram["xT"]).then_inc(s["inputs_landed"], 16)
            for i in range(4):
                sp.dma_start(ada_ring[:, i, :], dram["ada"][i]).then_inc(ada_landed[i], 16)
            for j in range(SLOTS):
                sp.dma_start(raw[:, j, 0:FULL], dram["even_in"][j]).then_inc(w_landed[j], 16)
            with sp.Fori(1, 6) as i:
                for r in range(4):
                    sp.wait_ge(s["ada_used"], 4 * i + (r - 3))
                    sp.dma_start(ada_ring[:, r, :], dram["ada"][4 * i + r]).then_inc(ada_landed[r], 16)
            done = 0
            for name, b0, turns, cols in stream:
                w = dram[name]
                first = 1 if done == 0 else 0
                with sp.Fori(first, turns) as i:
                    for j in range(SLOTS):
                        sp.wait_ge(s["lo_ready"], 2 * i + (done + j - 1))
                        sp.dma_start(raw[:, j, 0:cols], w[2 * i + (b0 + j)]).then_inc(w_landed[j], 16)
                done += SLOTS * turns
            sp.wait_ge(s["out_ready"], 4)
            sp.dma_start(out.rearrange("(t p) d -> p t d", p=P), arena[:, 0:4 * D].rearrange("p (t d) -> p t d", t=4)
                         ).then_inc(s["stored"], 16)
            sp.wait_ge(s["stored"], 16)

        def dve_link(dve, n, ins):
            ins.then_inc(s["dve_chain"], 1)
            dve.wait_ge(s["dve_chain"], n.add("dve_chain"))

        def act_link(act, n, ins):
            ins.then_inc(s["act_chain"], 1)
            act.wait_ge(s["act_chain"], n.add("act_chain"))

        def act_split(act, j, landed, cols):
            act.wait_ge(w_landed[j], landed)
            act.copy(w_hi[:, j, 0:cols], raw[:, j, 0:cols]).then_inc(s["hi_ready"], 1)

        def act_first_split(act, n):
            for j in range(SLOTS):
                act_split(act, j, 16, FULL)

        def act_feed(act, n, turns, consume=None):
            turn0, b0 = n.at("turn"), n.at("block_done")

            def turn(i, cols):
                for j in range(SLOTS):
                    act.wait_ge(s["block_done"], 2 * i + (b0 + j + 1))
                    if cols:
                        act_split(act, j, 16 * i + 16 * (turn0 + 2), cols)
                    if consume and j == 0:
                        consume(i)

            if turns > 1:
                with act.Fori(0, turns - 1) as i:
                    turn(i, ahead[turn0])
            turn(turns - 1, ahead[turn0 + turns - 1])

        def pool_feed(pool, n, turns, cols):
            b0 = n.at("block_done")
            with pool.Fori(0, turns) as i:
                for j in range(SLOTS):
                    pool.wait_ge(s["hi_ready"], 2 * i + (b0 + j + 1))
                    pool.tensor_tensor(w_lo[:, j, 0:cols], raw[:, j, 0:cols], w_hi[:, j, 0:cols].bitcast(F32), ALU.subtract
                                       ).then_inc(s["lo_ready"], 1)

        def pe_products(pe, j, hi, lo, halves, kt, fresh=None):
            for k in range(kt):
                if fresh is not None:
                    pe.wait_ge(s["parts_ready"], fresh + k + 1)
                w = slice(k * P, (k + 1) * P)
                for wt, acts in ((w_hi, hi), (w_hi, lo), (w_lo, hi)):
                    for b, (c0, cn) in enumerate(halves):
                        mm = pe.matmul(ps[:, 2 * j + b, 0:cn], wt[:, j, w], acts[:, k, c0:c0 + cn],
                                       start=(k == 0 and wt is w_hi and acts is hi), stop=(k == kt - 1 and wt is w_lo))
            mm.then_inc(s["block_done"], 1)

        def pe_project(pe, n, acts, halves, turns):
            hi, lo, kt = acts
            b0, read0 = n.at("block_done"), n.at("tile_read")
            fresh = n.pop("fresh", None)

            def turn(i, first=None):
                for j in range(SLOTS):
                    pe.wait_ge(s["lo_ready"], 2 * i + (b0 + j + 1))
                    pe.wait_ge(s["tile_read"], 2 * i + (read0 + j + 1))
                    pe_products(pe, j, hi, lo, halves, kt, first if j == 0 else None)

            if fresh is not None:
                turn(0, fresh)
            with pe.Fori(0 if fresh is None else 1, turns) as i:
                turn(i)

        def pe_gate_up(pe, n, halves):
            b0, read0, g0 = n.at("block_done"), n.at("tile_read"), n.at("gate_ready")
            pe.wait_ge(s["tile_read"], read0 + SLOTS)
            fresh = n.pop("fresh", None)

            def turn(i, first=None):
                pe.wait_ge(s["lo_ready"], 2 * i + (b0 + 1))
                pe.wait_ge(s["gate_ready"], i + (g0 + 1))
                pe_products(pe, 0, act_hi, act_lo, halves, KD, first)
                pe.wait_ge(s["lo_ready"], 2 * i + (b0 + 2))
                pe.wait_ge(s["tile_read"], 2 * i + (read0 + 2))
                pe_products(pe, 1, act_hi, act_lo, halves, KD)

            if fresh is not None:
                turn(0, fresh)
            with pe.Fori(0 if fresh is None else 1, 11) as i:
                turn(i)

        staged = raw[:, :, FULL:FULL + 3 * P]

        def pe_project_tok(pe, n, acts, tiles, turns):
            hi, lo, kt = acts
            b0, read0, t0 = n.at("block_done"), n.at("tile_read"), n.at("token_tiles")
            halves = token_halves(tiles)

            def turn(m):
                j = m % SLOTS
                pe.wait_ge(s["token_staged"], t0 + m + 1)
                if m >= 2:
                    pe.wait_ge(s["tile_read"], read0 + m + 1)
                for t, (c0, rows) in enumerate(tiles):
                    b = 1 if c0 >= halves[1][0] else 0
                    c = c0 - halves[b][0]
                    mm = pe.transpose(ps[0:rows, 4 + 2 * j + t // 4, (t % 4) * P:(t % 4 + 1) * P],
                                      staged[:, b, c:c + rows], ident)
                mm.then_inc(s["token_tiles"], 1)

            for m in range(SLOTS * turns):
                j = m % SLOTS
                pe.wait_ge(s["lo_ready"], b0 + m + 1)
                if m < 2:
                    pe.wait_ge(s["tile_read"], read0 + m + 1)
                else:
                    pe.wait_ge(s["token_staged"], t0 + m - 1)
                pe_products(pe, j, hi, lo, halves, kt)
                if m:
                    turn(m - 1)
            turn(SLOTS * turns - 1)

        def token_halves(tiles):
            return [(0, 3 * P), (3 * P, 3 * P)] if len(tiles) == NCH else [(TOK2, META + 2 * P), (TOK2 + META + 2 * P, 2 * P)]

        def dve_stage_tok(dve, n, tiles, m):
            b0, t0 = n.at("block_done"), n.at("token_tiles")
            dve.wait_ge(s["block_done"], b0 + m + 1)
            if m:
                dve.wait_ge(s["token_tiles"], t0 + m)
            for b, (c0, cn) in enumerate(token_halves(tiles)):
                ins = dve.tensor_copy(staged[:, b, 0:cn], ps[:, 2 * (m % SLOTS) + b, 0:cn])
            ins.then_inc(s["token_staged"], 1)

        def dve_copy_out(dve, n, halves, turns, dst, scale=None):
            b0 = n.at("block_done")
            with dve.Fori(0, turns) as i:
                for j in range(SLOTS):
                    dve.wait_ge(s["block_done"], 2 * i + (b0 + j + 1))
                    for b, (c0, cn) in enumerate(halves):
                        if scale is None:
                            ins = dve.tensor_copy(dst(2 * i + j, b), ps[:, 2 * j + b, 0:cn])
                        else:
                            ins = dve.tensor_scalar(dst(2 * i + j, b), ps[:, 2 * j + b, 0:cn], scale, None, ALU.mult)
                    ins.then_inc(s["tile_read"], 1)

        def dve_copy_tok(dve, n, tiles, turns, dst):
            last = SLOTS * turns
            for m in range(last + 1):
                if m < last:
                    dve_stage_tok(dve, n, tiles, m)
                if m == 0:
                    continue
                j = (m - 1) % SLOTS
                dve.wait_ge(s["token_tiles"], n.at("token_tiles") + m)
                f0 = (m - 1) * P
                src = ps[:, 4 + 2 * j:6 + 2 * j, :].rearrange("p a b -> p (a b)")
                full = len([t for t in tiles if t[1] == P])
                ins = dve.tensor_copy(dst[:, 0:full, f0:f0 + P],
                                      src[:, 0:full * P].rearrange("p (t f) -> p t f", f=P))
                if full < len(tiles):
                    rows = tiles[-1][1]
                    ins = dve.tensor_copy(dst[0:rows, full, f0:f0 + P], src[0:rows, full * P:full * P + P])
                ins.then_inc(s["tile_read"], 1)

        def dve_residual(dve, n, halves, turns, gate):
            b0 = n.at("block_done")
            with dve.Fori(0, turns) as i:
                for j in range(SLOTS):
                    dve.wait_ge(s["block_done"], 2 * i + (b0 + j + 1))
                    m = 2 * i + j
                    for b, (c0, cn) in enumerate(halves):
                        dst = x[:, m, c0:c0 + cn]
                        if gate is None:
                            ins = dve.tensor_tensor(dst, ps[:, 2 * j + b, 0:cn], dst, ALU.add)
                        else:
                            g = mod[:, gate + m, (1 if c0 == 0 else 0):(2 if c0 == 0 else 1)]
                            ins = dve.scalar_tensor_tensor(dst, ps[:, 2 * j + b, 0:cn], g, dst, ALU.mult, ALU.add)
                    ins.then_inc(s["tile_read"], 1)

        def act_gates(act, n, halves):
            r0 = n.at("tile_read")

            def silu(i):
                act.wait_ge(s["tile_read"], 2 * i + (r0 + 2))
                for b, (c0, cn) in enumerate(halves):
                    ins = act.activation(nscr[:, 0, c0:c0 + cn], ps[:, b, 0:cn], ACT.Silu)
                ins.then_inc(s["gate_ready"], 1)

            act_feed(act, n, 11, silu)

        def dve_gated(dve, n, halves):
            b0, g0, p0 = n.at("block_done"), n.at("gate_ready"), n.at("product_step")
            c0, c1 = halves[0][0], halves[-1][0] + halves[-1][1]
            product = nscr[:, 1, c0:c1]
            with dve.Fori(0, 11) as i:
                dve.wait_ge(s["block_done"], 2 * i + (b0 + 2))
                dve.wait_ge(s["gate_ready"], i + (g0 + 2))
                for b, (h0, hn) in enumerate(halves):
                    ins = dve.tensor_tensor(nscr[:, 1, h0:h0 + hn], nscr[:, 0, h0:h0 + hn], ps[:, 2 + b, 0:hn], ALU.mult)
                ins.then_inc(s["product_step"], 1)
                dve.wait_ge(s["product_step"], 2 * i + (p0 + 1))
                dve.tensor_copy(ff_hi[:, i, c0:c1], product).then_inc(s["product_step"], 1)
                dve.wait_ge(s["product_step"], 2 * i + (p0 + 2))
                dve.tensor_tensor(ff_lo[:, i, c0:c1], product, ff_hi[:, i, c0:c1].bitcast(F32), ALU.subtract
                                  ).then_inc(s["tile_read"], 2)

        def pe_down(pe, n, halves):
            pe.wait_ge(s["tile_read"], n.at("tile_read") + SLOTS)
            pe_project(pe, n, (ff_hi, ff_lo, SLOT_K), halves, 4)

        def act_norm(act, n, halves, a, shift, last):
            c0 = halves[0][0]
            end = halves[-1][0] + halves[-1][1]
            u0 = n.at("squares_used")
            for k in range(KD):
                if k >= 2:
                    act.wait_ge(s["squares_used"], u0 + k - 1)
                act.activation(nscr[:, k % 2, c0:end], x[:, k, c0:end], ACT.Square).then_inc(s["squares_ready"], 1)
            act.wait_ge(s["squares_used"], u0 + KD)
            for b, (h0, hn) in enumerate(halves):
                ins = act.activation(nscr[:, 2, h0:h0 + hn], ps[:, b, 0:hn], ACT.Sqrt, bias=eps_ap, scale=1.0 / D)
            ins.then_inc(s["roots_ready"], 1)
            if last:
                return
            for k in range(KD):
                act.wait_ge(s["scaled_ready"], n.at("scaled_ready") + k + 1)
                y = nscr[:, 4 + k % 2, :]
                if a is not None:
                    for b, (h0, hn) in enumerate(halves):
                        z = 1 if h0 == 0 else 0
                        ins = act.activation(y[:, h0:h0 + hn], y[:, h0:h0 + hn], ACT.Identity,
                                             bias=mod[:, shift + k, z:z + 1], scale=amod[:, a, k, z:z + 1])
                    act_link(act, n, ins)
                act.copy(act_hi[:, k, c0:end], y[:, c0:end]).then_inc(s["modulated"], 1)

        def pe_norm(pe, n, halves):
            for k in range(KD):
                pe.wait_ge(s["squares_ready"], n.at("squares_ready") + k + 1)
                for b, (h0, hn) in enumerate(halves):
                    mm = pe.matmul(ps[:, b, 0:hn], ones, nscr[:, k % 2, h0:h0 + hn], start=(k == 0), stop=(k == KD - 1))
                mm.then_inc(s["squares_used"], 1)

        def dve_norm(dve, n, halves, gain, last):
            c0 = halves[0][0]
            end = halves[-1][0] + halves[-1][1]
            dve.wait_ge(s["roots_ready"], n.at("roots_ready") + 1)
            dve_link(dve, n, dve.reciprocal(nscr[:, 3, c0:end], nscr[:, 2, c0:end]))

            def low(k):
                dve.wait_ge(s["modulated"], n.at("modulated") + k + 1)
                dve.tensor_tensor(act_lo[:, k, c0:end], nscr[:, 4 + k % 2, c0:end],
                                  act_hi[:, k, c0:end].bitcast(F32), ALU.subtract).then_inc(s["parts_ready"], 1)
                dve.wait_ge(s["parts_ready"], n.at("parts_ready") + k + 1)

            for k in range(KD):
                if last:
                    dve.scalar_tensor_tensor(mix[:, k, c0:end], x[:, k, c0:end], gain(k), nscr[:, 3, c0:end],
                                             ALU.mult, ALU.mult)
                    continue
                if k >= 2:
                    low(k - 2)
                y = nscr[:, 4 + k % 2, c0:end]
                if gain is None:
                    ins = dve.tensor_tensor(y, x[:, k, c0:end], nscr[:, 3, c0:end], ALU.mult)
                else:
                    ins = dve.scalar_tensor_tensor(y, x[:, k, c0:end], gain(k), nscr[:, 3, c0:end], ALU.mult, ALU.mult)
                ins.then_inc(s["scaled_ready"], 1)
            if not last:
                low(KD - 2)
                low(KD - 1)

        def act_mix_parts(act, n, halves):
            c0, c1 = halves[0][0], halves[-1][0] + halves[-1][1]
            for k in range(KD):
                act.copy(act_hi[:, k, c0:c1], mix[:, k, c0:c1]).then_inc(s["mix_hi"], 1)

        def dve_mix_parts(dve, n, halves):
            c0, c1 = halves[0][0], halves[-1][0] + halves[-1][1]
            for k in range(KD):
                dve.wait_ge(s["mix_hi"], n.at("mix_hi") + k + 1)
                dve.tensor_tensor(act_lo[:, k, c0:c1], mix[:, k, c0:c1], act_hi[:, k, c0:c1].bitcast(F32), ALU.subtract
                                  ).then_inc(s["parts_ready"], 1)

        def halves_of(cols):
            return [(0, cols // 2), (cols // 2, cols // 2)] if cols > 512 else [(0, cols)]

        def act_head_norm(act, n, tiles, matrix, scale, rope):
            q0, r0, d0 = n.at("sums_ready"), n.at("roots_ready"), n.at("head_scaled")

            def root(i):
                cols = tiles[i][3]
                act.wait_ge(s["sums_ready"], q0 + i + 1)
                if i >= 2:
                    act.wait_ge(s["head_scaled"], d0 + i - 1)
                for b, (c0, cn) in enumerate(halves_of(cols)):
                    ins = act.activation(scr[:, 2 + i % 2, c0:c0 + cn], ps[:, 2 * (i % 2) + b, 0:cn], ACT.Sqrt,
                                         bias=eps_ap, scale=scale)
                ins.then_inc(s["roots_ready"], 1)

            for i, (src, dst, gain, cols) in enumerate(tiles):
                if i >= 2:
                    act.wait_ge(s["sums_ready"], q0 + i - 1)
                act.activation(scr[:, i % 2, 0:cols], src, ACT.Square).then_inc(s["squares_ready"], 1)
                if i >= 1:
                    root(i - 1)
            root(len(tiles) - 1)

        def pe_head_norm(pe, n, tiles, matrix, scale, rope):
            for i, (src, dst, gain, cols) in enumerate(tiles):
                pe.wait_ge(s["squares_ready"], n.at("squares_ready") + i + 1)
                if i >= 2:
                    pe.wait_ge(s["roots_ready"], n.at("roots_ready") + i - 1)
                for b, (c0, cn) in enumerate(halves_of(cols)):
                    mm = pe.matmul(ps[:, 2 * (i % 2) + b, 0:cn], matrix, scr[:, i % 2, c0:c0 + cn], start=True, stop=True)
                mm.then_inc(s["sums_ready"], 1)

        def dve_head_norm(dve, n, tiles, matrix, scale, rope):
            for i, (src, dst, gain, cols) in enumerate(tiles):
                dve.wait_ge(s["roots_ready"], n.at("roots_ready") + i + 1)
                r = scr[:, 2 + i % 2, 0:cols]
                dve_link(dve, n, dve.reciprocal(r, r))
                ins = dve.scalar_tensor_tensor(dst, src, gain, r, ALU.mult, ALU.mult)
                ins.then_inc(s["head_scaled"], 1)
                if rope:
                    y = dst[:, CTX:T] if cols == T else dst
                    dve.wait_ge(s["head_scaled"], n.at("head_scaled") + i + 1)
                    dve_link(dve, n, dve.stream_shuffle(scr[:, 4, 0:LAT], y, [j ^ 1 for j in range(32)]))
                    dve.tensor_tensor(scr[:, 5, 0:LAT], y, pa[:, 0:LAT], ALU.mult)
                    dve_link(dve, n, dve.tensor_tensor(scr[:, 4, 0:LAT], scr[:, 4, 0:LAT], pa[:, LAT:2 * LAT], ALU.mult))
                    dve_link(dve, n, dve.tensor_tensor(y, scr[:, 4, 0:LAT], scr[:, 5, 0:LAT], ALU.add))

        def score_banks(m, u, maps):
            return 2 * (m if maps == 2 else u % 2)

        def exp_row(u, m, maps):
            return 2 * (u % 2) + m if maps == 2 else u % 2

        def pe_attend(pe, n, units, maps, bias):
            U = len(units)

            def scores(u):
                w = units[u]
                for m in range(maps):
                    g = u * maps + m
                    if g >= 2:
                        name = "bias_ready" if bias else "exp_done"
                        pe.wait_ge(s[name], n.at(name) + g - 1)
                    for b, k0, kn in w["segs"]:
                        mm = pe.matmul(ps[0:w["nq"], score_banks(m, u, maps) + b, 0:kn], w["q"][m], w["k"][m][:, k0:k0 + kn],
                                       start=True, stop=True)
                    mm.then_inc(s["scores_ready"], 1)

            def turn(u):
                w = units[u]
                pe.wait_ge(s["p_ready"], n.at("p_ready") + u + 1)
                if u >= 1:
                    pe.wait_ge(s["pt_copied"], n.at("pt_copied") + u)
                for t, (c0, rows) in enumerate(w["keys"]):
                    if maps == 1:
                        mm = pe.transpose(ps[0:rows, 4 + t // 4, (t % 4) * P:(t % 4) * P + w["nq"]],
                                          scr[0:w["nq"], w["p"], c0:c0 + rows], ident[0:w["nq"], 0:w["nq"]])
                        continue
                    for m in range(maps):
                        mm = pe.matmul(ps[0:rows, 4 + t // 4, (t % 4) * P:(t % 4) * P + w["nq"]],
                                       scr[0:w["nq"], exp_row(u, m, maps), c0:c0 + rows], diags[0:w["nq"], u % 2, m, 0:w["nq"]],
                                       start=(m == 0), stop=(m == maps - 1))
                mm.then_inc(s["pt_psum"], 1)

            def weigh(u):
                w = units[u]
                pe.wait_ge(s["pt_copied"], n.at("pt_copied") + u + 1)
                if u >= 2:
                    pe.wait_ge(s["o_read"], n.at("o_read") + u - 1)
                o0, on = w["o_part"]
                for t, (c0, rows) in enumerate(w["keys"]):
                    mm = pe.matmul(ps[o0:o0 + on, 6 + u % 2, 0:w["nq"]], w["v"][t],
                                   scr[0:rows, 4 + u % 2, t * P:t * P + w["nq"]],
                                   start=(t == 0), stop=(t == len(w["keys"]) - 1))
                mm.then_inc(s["pv_done"], 1)

            scores(0)
            for st in range(U + 2):
                if maps == 1 and st + 1 < U:
                    scores(st + 1)
                if 1 <= st <= U:
                    turn(st - 1)
                if st >= 2:
                    weigh(st - 2)
                if maps == 2 and st + 1 < U:
                    scores(st + 1)

        def act_attend(act, n, units, maps, bias):
            U = len(units)
            for st in range(U + 1):
                if st < U:
                    w = units[st]
                    for m in range(maps):
                        g = st * maps + m
                        act.wait_ge(s["bias_ready"], n.at("bias_ready") + g + 1)
                        if bias:
                            z = scr[0:w["nq"], w["p"], 0:w["nk"]]
                            src = z
                        else:
                            z = scr[0:w["nq"], exp_row(st, m, maps), 0:w["nk"]]
                            c = w["segs"][0][2]
                            src = ps[0:w["nq"], 2 * m:2 * m + 2, 0:c]
                            z = z.rearrange("p (a b) -> p a b", a=2)
                            if st >= 2:
                                act.wait_ge(s["pt_psum"], n.at("pt_psum") + st - 1)
                        act.activation(z, src, ACT.Exp, bias=small[0:w["nq"], g % 4:g % 4 + 1], scale=1.0,
                                       accum_out=small[0:w["nq"], 4 + g % 4:5 + g % 4]).then_inc(s["exp_done"], 1)
                if st >= 1:
                    u = st - 1
                    w = units[u]
                    act.wait_ge(s["pt_psum"], n.at("pt_psum") + u + 1)
                    if u >= 2:
                        act.wait_ge(s["pv_done"], n.at("pv_done") + u - 1)
                    nt, nq = len(w["keys"]), w["nq"]
                    whole = [t for t in range(nt) if w["keys"][t][1] == P]
                    for bank in (0, 1):
                        ts = [t for t in whole if t // 4 == bank]
                        if ts:
                            a, z = ts[0], ts[-1] + 1
                            ins = act.copy(scr[:, 4 + u % 2, a * P:z * P].rearrange("p (t q) -> p t q", q=P)[:, :, 0:nq],
                                           ps[:, 4 + bank, (a % 4) * P:(a % 4 + z - a) * P].rearrange(
                                               "p (t q) -> p t q", q=P)[:, :, 0:nq])
                    for t in range(nt):
                        rows = w["keys"][t][1]
                        if rows != P:
                            ins = act.copy(scr[0:rows, 4 + u % 2, t * P:t * P + nq],
                                           ps[0:rows, 4 + t // 4, (t % 4) * P:(t % 4) * P + nq])
                    ins.then_inc(s["pt_copied"], 1)

        def dve_attend(dve, n, units, maps, bias):
            U = len(units)

            def shift(u):
                w = units[u]
                nq = w["nq"]
                for m in range(maps):
                    g = u * maps + m
                    dve.wait_ge(s["scores_ready"], n.at("scores_ready") + g + 1)
                    top = small[0:nq, g % 4:g % 4 + 1]
                    if not bias:
                        c = w["segs"][0][2]
                        dve.tensor_reduce(top, ps[0:nq, 2 * m:2 * m + 2, 0:c], AX.XY, ALU.max, negate=True
                                          ).then_inc(s["bias_ready"], 1)
                        continue
                    if u >= 2:
                        dve.wait_ge(s["pt_psum"], n.at("pt_psum") + u - 1)
                    z = scr[0:nq, w["p"], 0:w["nk"]]
                    for b, k0, kn in w["segs"]:
                        src = ps[0:nq, 2 * (u % 2) + b, 0:kn]
                        kind, arg = w["bias"][b]
                        if kind == "plain":
                            ins = dve.tensor_copy(z[:, k0:k0 + kn], src)
                        elif kind == "table":
                            ins = dve.tensor_tensor(z[:, k0:k0 + kn], src, arg, ALU.add)
                        else:
                            ins = dve.scalar_tensor_tensor(z[:, k0:k0 + kn], src, arg[0], arg[1][:, k0:k0 + kn],
                                                           ALU.add, ALU.add)
                    dve_link(dve, n, ins)
                    if w["diag"] is not None:
                        d = z[:, w["diag"]:w["diag"] + nq]
                        dve_link(dve, n, dve.tensor_tensor(d, d, dmask[0:nq, 0:nq], ALU.add))
                    dve.tensor_reduce(top, z, AX.X, ALU.max, negate=True).then_inc(s["bias_ready"], 1)

            def normalise(u):
                w = units[u]
                nq = w["nq"]
                dve.wait_ge(s["exp_done"], n.at("exp_done") + maps * (u + 1))
                g = u * maps
                sums = small[0:nq, 4 + g % 4:4 + g % 4 + maps]
                inv = small[0:nq, 8 + 2 * (u % 2):8 + 2 * (u % 2) + maps]
                both = small[0:nq, 12 + u % 2:13 + u % 2]
                dve_link(dve, n, dve.reciprocal(inv, sums))
                eye = ident[0:nq, 0:nq]
                if maps == 1:
                    z = scr[0:nq, w["p"], 0:w["nk"]]
                    dve.tensor_scalar(z, z, inv[:, 0:1], None, ALU.mult).then_inc(s["p_ready"], 1)
                    return
                if u >= 2:
                    dve.wait_ge(s["pt_psum"], n.at("pt_psum") + u - 1)
                dve.tensor_scalar(diags[0:nq, u % 2, 0, 0:nq], eye, inv[:, 0:1], None, ALU.mult)
                dve_link(dve, n, dve.tensor_tensor(both, inv[:, 1:2], small[0:nq, 16:17], ALU.mult))
                dve.tensor_scalar(diags[0:nq, u % 2, 1, 0:nq], eye, both, None, ALU.mult).then_inc(s["p_ready"], 1)

            def take(u):
                w = units[u]
                o0, on = w["o_part"]
                dve.wait_ge(s["pv_done"], n.at("pv_done") + u + 1)
                dve.tensor_copy(w["out"], ps[o0:o0 + on, 6 + u % 2, 0:w["nq"]]).then_inc(s["o_read"], 1)

            for st in range(U + 3):
                if maps == 2 and 1 <= st <= U:
                    normalise(st - 1)
                if st < U:
                    shift(st)
                if maps == 1 and 1 <= st <= U:
                    normalise(st - 1)
                if 3 <= st:
                    take(st - 3)

        def act_setup(act, n):
            act.wait_ge(s["inputs_landed"], 64)
            act.sem_inc(s["tile_read"], 2)
            act.sem_inc(s["gate_ready"], 1)
            act.sem_inc(s["ada_read"], 4)
            act.sem_inc(s["ada_rows"], 4)
            act_link(act, n, act.activation(csil[:, :, :], v("c", 0, 16).rearrange("p (k z) -> p k z", k=KD), ACT.Silu))
            act.wait_ge(s["setup_ready"], 1)
            act.activation(small[:, 18:20], small[:, 18:20], ACT.Exp).then_inc(s["setup_ready"], 1)

        def dve_setup(dve, n):
            dve.wait_ge(s["inputs_landed"], 64)
            dve.memset(eps_t[:, :], EPS)
            dve.memset(small[:, 20:96], 0.0)
            lam = v("lam", 0, 256).rearrange("p (a d) -> p a d", a=4)
            prod = scr[:, 0, 0:128].rearrange("p (a d) -> p a d", a=2)
            dve_link(dve, n, dve.tensor_tensor(prod[:, 0:1, :], lam[:, 0:1, :], lam[:, 1:2, :], ALU.mult))
            dve_link(dve, n, dve.tensor_tensor(prod[:, 1:2, :], lam[:, 2:3, :], lam[:, 3:4, :], ALU.mult))
            dve.tensor_reduce(small[:, 18:20], prod, AX.X, ALU.add).then_inc(s["setup_ready"], 1)
            dve.wait_ge(s["setup_ready"], 2)
            dve_link(dve, n, dve.tensor_tensor(small[:, 16:17], small[:, 19:20], small[:, 18:19], ALU.subtract))
            dve_link(dve, n, dve.tensor_scalar(small[:, 16:17], small[:, 16:17], -LAM_INIT, None, ALU.add))
            dve.tensor_scalar(v("diff_gain"), v("diff_gain"), 64 ** -0.5, None, ALU.mult)
            dve.tensor_scalar(v("na_gain"), v("na_gain"), 128 ** -0.5, None, ALU.mult)
            dve.tensor_scalar(v("subln"), v("subln"), 1.0 - LAM_INIT, None, ALU.mult)

        LAM_INIT = 0.8 - 0.6 * math.exp(0.0)

        ada_rows = nscr[0:2, 0:4, 0:4 * P]

        def pe_ada(pe, n):
            pe.wait_ge(s["act_chain"], 1)
            with pe.Fori(0, 6) as i:
                def products(r):
                    pe.wait_ge(ada_landed[r], 16 * i + 16)
                    pe.wait_ge(s["ada_rows"], 4 * i + (r + 1))
                    w = ada_ring[:, r, :].rearrange("p (q k o) -> p k q o", q=4, k=KD)
                    for k in range(KD):
                        mm = pe.matmul(ps[0:2, r, :].rearrange("p (q o) -> p q o", q=4), csil[:, k, :], w[:, k],
                                       start=(k == 0), stop=(k == KD - 1))
                    mm.then_inc(s["ada_used"], 1)

                def turn(r):
                    pe.wait_ge(s["ada_rows"], 4 * i + (r + 5))
                    pe.wait_ge(s["ada_read"], 4 * i + (r + 1))
                    for q in range(4):
                        mm = pe.matmul(ps[:, 4 + r, 2 * q:2 * q + 2], ada_rows[:, r, q * P:(q + 1) * P], ident[0:2, 0:2], start=True, stop=True)
                    mm.then_inc(s["ada_turned"], 1)

                products(0)
                for r in range(1, 4):
                    products(r)
                    turn(r - 1)
                turn(3)

        def act_ada(act, n):
            with act.Fori(0, 6) as i:
                for r in range(4):
                    act.wait_ge(s["ada_used"], 4 * i + (r + 1))
                    act.copy(ada_rows[:, r, :], ps[0:2, r, :]).then_inc(s["ada_rows"], 1)

        def dve_ada(dve, n):
            with dve.Fori(0, 6) as i:
                for r in range(4):
                    dve.wait_ge(s["ada_turned"], 4 * i + (r + 1))
                    b = vec[:, VEC["ada_b"]:VEC["ada_b"] + 96].rearrange("p (g q) -> p g q", q=4)[:, 4 * i + r, :]
                    m = mod[:, :, :].rearrange("p (g q) z -> p g (q z)", q=4)[:, 4 * i + r, :]
                    dve.tensor_tensor(m.rearrange("p (q z) -> p q z", z=2), ps[:, 4 + r, 0:8].rearrange("p (q z) -> p q z", z=2),
                                      b.unsqueeze(2).to_broadcast([P, 4, 2]), ALU.add).then_inc(s["ada_read"], 1)
            dve.wait_ge(s["ada_read"], 4 + 24)
            for l in range(2):
                for f, name in ((0, "norm_mix"), (1, "norm_ffn")):
                    sc = mod[:, 48 * l + 24 * f + 8:48 * l + 24 * f + 16, :]
                    g = v(name, 8 * l, 8).unsqueeze(2).to_broadcast([P, KD, 2])
                    dve.scalar_tensor_tensor(amod[:, 2 * l + f, :, :], sc, 1.0, g, ALU.add, ALU.mult)

        gd = arena[:, A_GD:A_GD + 16 * GW].rearrange("p (m t) -> p m t", m=16)
        GN = GW - 4

        def dve_conv(dve, n):
            for m in range(12):
                acc = scr[:, 4 + m % 2, 0:GN]
                w = lambda j: v("conv", 5 * m + j)
                dve.wait_ge(s["conv_first"], m + 1)
                for j in range(1, 5):
                    ins = dve.scalar_tensor_tensor(acc, gd[:, m, j:j + GN], w(j), acc, ALU.mult, ALU.add)
                    if j < 4:
                        dve_link(dve, n, ins)
                ins.then_inc(s["conv_ready"], 1)

        def act_conv(act, n):
            def first_tap(m):
                act.mul(scr[:, 4 + m % 2, 0:GN], gd[:, m, 0:GN], v("conv", 5 * m)).then_inc(s["conv_first"], 1)

            first_tap(0)
            first_tap(1)
            for m in range(12):
                act.wait_ge(s["conv_ready"], m + 1)
                act.activation(gd[:, m, 2:2 + CTX], scr[:, 4 + m % 2, 0:CTX], ACT.Silu)
                act.activation(gd[:, m, 260:260 + LAT], scr[:, 4 + m % 2, 258:258 + LAT], ACT.Silu
                               ).then_inc(s["conv_used"], 1)
                if m + 2 < 12:
                    act.wait_ge(s["conv_used"], m + 1)
                    first_tap(m + 2)

        la = gates[:, 0]
        beta = gates[:, 1]
        egrt = gates[:, 2:5]
        kscale = gates[:, 5]

        def by_dir(tab):
            return tab.rearrange("p (s d h) -> p d s h", s=6, d=2)

        def step_bc(tab, st):
            return tab[:, 8 * st:8 * st + 8].unsqueeze(2).to_broadcast([P, 8, P])

        ws_hi = w_hi[:, 0, FULL:FULL + KD * 16].rearrange("p (k g) -> p k g", k=KD)
        ws_lo = w_lo[:, 0, FULL:FULL + KD * 16].rearrange("p (k g) -> p k g", k=KD)

        def act_small_split(act, n, landed, cols):
            act.wait_ge(s["small_landed"], landed)
            act.copy(ws_hi[:, :, 0:cols], wsmall[:, :, 0:cols]).then_inc(s["small_hi"], 1)

        def dve_small_split(dve, n, landed, cols):
            dve.wait_ge(s["small_hi"], n.at("small_parts") + 1)
            dve.tensor_tensor(ws_lo[:, :, 0:cols], wsmall[:, :, 0:cols], ws_hi[:, :, 0:cols].bitcast(F32), ALU.subtract
                              ).then_inc(s["small_parts"], 1)

        def pe_small_products(pe, n, cols, halves):
            pe.wait_ge(s["small_parts"], n.at("small_parts"))
            for b, (c0, cn) in enumerate(halves):
                for k in range(KD):
                    for w, a in ((ws_hi, act_hi), (ws_hi, act_lo), (ws_lo, act_hi)):
                        mm = pe.matmul(ps[0:cols, b, 0:cn], w[:, k, 0:cols], a[:, k, c0:c0 + cn],
                                       start=(k == 0 and w is ws_hi and a is act_hi), stop=(k == KD - 1 and w is ws_lo))
            return mm

        def pe_gates_raw(pe, n):
            pe_small_products(pe, n, 16, [(0, 3 * P), (3 * P, 3 * P)]).then_inc(s["gates_rows"], 1)
            pe.wait_ge(s["gates_staged"], 1)
            for c in range(NCH):
                mm = pe.transpose(ps[:, 2, 16 * c:16 * c + 16], scr[0:16, 0, c * P:(c + 1) * P], ident[0:16, 0:16])
            mm.then_inc(s["step_pe"], 1)

        def dve_gates_raw(dve, n):
            for c in (0, 2 + CTX, GW - 2):
                dve.memset(gd[:, :, c:c + 2], 0.0)
            dve.wait_ge(s["gates_rows"], 1)
            dve.tensor_copy(scr[0:16, 0, 0:T].rearrange("p (a t) -> p a t", a=2), ps[0:16, 0:2, 0:3 * P]
                            ).then_inc(s["gates_staged"], 1)
            dve.wait_ge(s["step_pe"], 1)
            for st in range(6):
                for d, c in ((0, FWD[st]), (1, BWD[st])):
                    o = 8 * st + 4 * d
                    dve.tensor_copy(beta[:, o:o + 4], ps[:, 2, 16 * c + 4 * d:16 * c + 4 * d + 4])
                    dve.tensor_copy(la[:, o:o + 4], ps[:, 2, 16 * c + 8 + 4 * d:16 * c + 8 + 4 * d + 4])

        def dve_gates(dve, n):
            t0, t1 = gates[:, 6], gates[:, 7]
            shp = [P, 6, 8]
            cube = lambda a: a.rearrange("p (s e) -> p s e", e=8)
            dve.tensor_tensor(cube(la), cube(la), v("dt_bias", 0, 8).unsqueeze(1).to_broadcast(shp), ALU.add
                              ).then_inc(s["step_dve"], 1)
            dve.wait_ge(s["step_act"], 2)
            dve_link(dve, n, dve.tensor_scalar(beta, beta, 1.0, None, ALU.add))
            dve_link(dve, n, dve.reciprocal(beta, beta))
            dve_link(dve, n, dve.scalar_tensor_tensor(la, la, 0.0, t0, ALU.max, ALU.add))
            dve.scalar_tensor_tensor(cube(la), cube(la), -1.0, small[:, 20:28].unsqueeze(1).to_broadcast(shp),
                                     ALU.mult, ALU.mult).then_inc(s["step_dve"], 1)
            dve.wait_ge(s["step_act"], 3)
            dve.tensor_tensor(kscale, beta, gates[:, 3], ALU.mult)

        def act_gates_tab(act, n):
            t0 = gates[:, 6]
            act.activation(beta, beta, ACT.Exp, scale=-1.0)
            act.activation(small[:, 20:28], v("a_log", 0, 8), ACT.Exp)
            act.wait_ge(s["step_dve"], 1)
            act_link(act, n, act.activation(t0, la, ACT.Abs))
            act_link(act, n, act.activation(t0, t0, ACT.Exp, scale=-1.0))
            act.activation(t0, t0, ACT.Ln, bias=1.0).then_inc(s["step_act"], 2)
            act.wait_ge(s["step_pe"], 2)
            act.activation(gates[:, 2:5].rearrange("p a (s d h) -> p a d s h", s=6, d=2)[:, 0], ps[:, 0, 0:48].rearrange("p (d s h) -> p d s h", d=2, s=6), ACT.Exp)
            act.activation(gates[:, 3].rearrange("p (s d h) -> p d s h", s=6, d=2), ps[:, 0, 48:96].rearrange("p (d s h) -> p d s h", d=2, s=6), ACT.Exp)
            act.activation(gates[:, 4].rearrange("p (s d h) -> p d s h", s=6, d=2), ps[:, 0, 96:144].rearrange("p (d s h) -> p d s h", d=2, s=6), ACT.Exp
                           ).then_inc(s["step_act"], 1)

        def pe_gates_tab(pe, n):
            pe.wait_ge(s["tables_landed"], 32)
            pe.wait_ge(s["step_dve"], 2)
            for d in range(2):
                r = by_dir(la)[:, d]
                for kind, m in ((0, mask(2 + d)), (1, mask(d)), (2, ones)):
                    mm = pe.matmul(ps[:, 0, 48 * kind + 24 * d:48 * kind + 24 * d + 24], m, r, start=True, stop=True)
            mm.then_inc(s["step_pe"], 1)

        def mask(i):
            return pb_[:, i * P:(i + 1) * P]

        def masks(i):
            return pb_[:, i * P:(i + 2) * P].rearrange("p (d t) -> p d t", d=2).unsqueeze(2).to_broadcast([P, 2, 4, P])

        bufs = [arena[:, 1024 * i:1024 * (i + 1)] for i in range(6)]
        flat = sb("delta_bufs", [P, 6 * 1024], F32, "act_hi")
        bufs += [flat[:, 1024 * i:1024 * (i + 1)] for i in range(6)]
        (NT, AQ, LAM_KE, LAB_B, DEC_B, QG, Y, X, XT, KT, VT, ST) = bufs
        oacc = mix[:, 4:8, :]
        PE_MARKS = ["kk", "kq", "kt", "vt", "decay", "row", "y0"] + [f"{a}{l}{d}" for l in range(1, 7) for a in "yx" for d in "fb"] + \
            ["wt", "u", "o", "ds"]
        ACT_MARKS = ["kk", "kt", "vt", "decay", "row"] + [f"y{l}{d}" for l in range(1, 7) for d in "fb"] + ["u"]
        DVE_MARKS = ["kq", "aq", "nt", "xt0", "x0"] + [f"x{l}{d}" for l in range(1, 7) for d in "fb"] + ["qg", "wt", "o", "s"]
        POOL_MARKS = ["lam", "lab"] + [f"b{l}" for l in range(1, 7)] + ["ke", "kg"]
        MARKS = {"pe": (PE_MARKS, 2), "act": (ACT_MARKS, 3), "dve": (DVE_MARKS, 2), "pool": (POOL_MARKS, 0)}

        WAYS = list(enumerate("fb"))

        def way(buf, d):
            return buf[:, 4 * P * d:4 * P * (d + 1)]

        def after(eng, who, st, mark):
            marks, start = MARKS[who]
            eng.wait_ge(s["step_" + who], start + len(marks) * st + marks.index(mark) + 1)

        def pair(b):
            return ps[:, b:b + 2, :].rearrange("p a t -> p (a t)")

        def sq(buf, d, hd):
            return buf[:, (4 * d + hd) * P:(4 * d + hd + 1) * P]

        def bank(b, d, hd):
            return ps[:, b + d, hd * P:(hd + 1) * P]

        EIGHT = [(d, hd) for d in range(2) for hd in range(4)]

        def chunk(tile, st, d):
            c = CH_COL[(FWD, BWD)[d][st]]
            return gd[:, tile, c:c + P]

        def pe_delta(pe, n):
            inc = lambda mm: mm.then_inc(s["step_pe"], 1)
            for st in range(6):
                if st:
                    after(pe, "act", st - 1, "u")
                for d, e in EIGHT:
                    mm = pe.matmul(bank(0, d, e), chunk(4 + e, st, d), chunk(4 + e, st, d), start=True, stop=True)
                inc(mm)
                if st:
                    after(pe, "dve", st - 1, "o")
                for d, e in EIGHT:
                    mm = pe.matmul(bank(2, d, e), chunk(4 + e, st, d), chunk(e, st, d), start=True, stop=True)
                inc(mm)
                if st:
                    after(pe, "dve", st - 1, "s")
                for d, e in EIGHT:
                    mm = pe.transpose(bank(4, d, e), chunk(4 + e, st, d), ident)
                inc(mm)
                for d, e in EIGHT:
                    mm = pe.transpose(bank(6, d, e), chunk(8 + e, st, d), ident)
                inc(mm)
                after(pe, "act", st, "kk")
                after(pe, "pool", st, "lam")
                for d, e in EIGHT:
                    mm = pe.matmul(bank(0, d, e), sq(LAM_KE, d, e), mask(2 + d), start=True, stop=True)
                inc(mm)
                after(pe, "dve", st, "kq")
                after(pe, "pool", st, "lab")
                for d, e in EIGHT:
                    mm = pe.matmul(bank(2, d, e), sq(LAB_B, d, e), mask(2 + d), start=True, stop=True)
                inc(mm)
                after(pe, "act", st, "decay")
                after(pe, "dve", st, "xt0")
                for d, e in EIGHT:
                    mm = pe.transpose(bank(0, d, e), sq(LAB_B, d, e), ident)
                inc(mm)
                for l in range(1, 7):
                    for d, name in WAYS:
                        after(pe, "dve", st, f"x{l - 1}{name}" if l > 1 else "x0")
                        if d == 0:
                            after(pe, "pool", st, f"b{l}")
                            if l == 1:
                                after(pe, "act", st, "row")
                        for e in range(4):
                            mm = pe.matmul(bank(2, d, e), sq(DEC_B if l % 2 else LAB_B, d, e), sq(X, d, e), start=True, stop=True)
                        inc(mm)
                    for d, name in WAYS:
                        after(pe, "act", st, f"y{l}{name}")
                        for e in range(4):
                            mm = pe.matmul(bank(0, d, e), sq(Y, d, e), sq(XT, d, e), start=True, stop=True)
                        if l < 6:
                            for e in range(4):
                                mm = pe.matmul(bank(4, d, e), sq(XT, d, e), sq(Y, d, e), start=True, stop=True)
                        inc(mm)
                after(pe, "dve", st, "x6b")
                after(pe, "pool", st, "ke")
                after(pe, "act", st, "vt")
                for d, e in EIGHT:
                    mm = pe.matmul(bank(6, d, e), sq(LAM_KE, d, e), sq(XT, d, e), start=True, stop=True)
                inc(mm)
                after(pe, "dve", st, "wt")
                for d, e in EIGHT:
                    pe.matmul(bank(0, d, e), sq(XT, d, e), sq(VT, d, e), start=True, stop=False)
                    mm = pe.matmul(bank(0, d, e), sq(Y, d, e), sq(ST, d, e), start=False, stop=True)
                inc(mm)
                after(pe, "act", st, "u")
                for d, e in EIGHT:
                    pe.matmul(bank(2, d, e), sq(ST, d, e), sq(QG, d, e), start=True, stop=False)
                    mm = pe.matmul(bank(2, d, e), sq(X, d, e), sq(AQ, d, e), start=False, stop=True)
                inc(mm)
                after(pe, "pool", st, "kg")
                for d, e in EIGHT:
                    mm = pe.matmul(bank(4, d, e), sq(KT, d, e), sq(X, d, e), start=True, stop=True)
                inc(mm)

        def act_delta(act, n):
            for st in range(6):
                def take(mark, dst, b, f=ACT.Copy):
                    after(act, "pe", st, mark)
                    act.activation(dst, pair(b), f).then_inc(s["step_act"], 1)
                take("kk", NT, 0)
                take("kt", KT, 4)
                take("vt", VT, 6)
                take("decay", DEC_B, 0, ACT.Exp)
                take("row", QG, 2, ACT.Exp)
                for l in range(1, 7):
                    for d, name in WAYS:
                        after(act, "pe", st, f"y{l}{name}")
                        act.activation(way(Y, d), ps[:, 2 + d, :], ACT.Copy).then_inc(s["step_act"], 1)
                take("u", X, 0)

        def dve_delta(dve, n):
            inc = lambda ins: ins.then_inc(s["step_dve"], 1)
            quad = lambda b: b.rearrange("p (d h t) -> p d h t", d=2, h=4)
            eight = lambda b: b.rearrange("p (e t) -> p e t", e=8)
            eye = ident.unsqueeze(1).to_broadcast([P, 8, P])
            dve.memset(ST, 0.0)
            dve.memset(oacc, 0.0)
            for st in range(6):
                after(dve, "pe", st, "kq")
                inc(dve.tensor_copy(AQ, pair(2)))
                after(dve, "act", st, "decay")
                dve_link(dve, n, dve.tensor_tensor(eight(DEC_B), eight(DEC_B), step_bc(beta, st), ALU.mult))
                dve_link(dve, n, dve.tensor_tensor(quad(DEC_B), quad(DEC_B), masks(2), ALU.mult))
                inc(dve.tensor_tensor(AQ, AQ, DEC_B, ALU.mult))
                inc(dve.tensor_tensor(NT, NT, DEC_B, ALU.mult))
                after(dve, "dve", st, "nt")
                after(dve, "pe", st, "row")
                dve_link(dve, n, dve.tensor_tensor(quad(LAB_B), quad(NT), masks(4), ALU.mult))
                inc(dve.scalar_tensor_tensor(eight(XT), eight(LAB_B), -1.0, eye, ALU.mult, ALU.add))
                after(dve, "pe", st, "y0")
                inc(dve.scalar_tensor_tensor(eight(X), eight(pair(0)), -1.0, eye, ALU.mult, ALU.add))
                for l in range(1, 7):
                    for d, name in WAYS:
                        after(dve, "pe", st, f"x{l}{name}")
                        after(dve, "dve", st, f"x{l - 1}{name}" if l > 1 else "x0")
                        ins = dve.tensor_tensor(way(XT, d), way(XT, d), ps[:, d, :], ALU.subtract)
                        if l < 6:
                            ins = dve.tensor_tensor(way(X, d), way(X, d), ps[:, 4 + d, :], ALU.subtract)
                        inc(ins)
                after(dve, "act", st, "row")
                for d in range(2):
                    c = CH_COL[(FWD, BWD)[d][st]]
                    ins = dve.tensor_tensor(quad(QG)[:, d], quad(QG)[:, d], gd[:, 0:4, c:c + P], ALU.mult)
                inc(ins)
                after(dve, "pe", st, "wt")
                inc(dve.tensor_scalar(Y, pair(6), -1.0, None, ALU.mult))
                after(dve, "pe", st, "o")
                for d in range(2):
                    c = (FWD, BWD)[d][st] * P
                    o = oacc[:, :, c:c + P]
                    dve_link(dve, n, dve.tensor_tensor(o, o, ps[:, 2 + d, :].rearrange("p (h t) -> p h t", h=4), ALU.add))
                dve.tensor_copy(small[:, 30:31], small[:, 32:33]).then_inc(s["step_dve"], 1)
                dve_link(dve, n, dve.tensor_tensor(eight(ST), eight(ST), step_bc(gates[:, 4], st), ALU.mult))
                after(dve, "pe", st, "ds")
                ins = dve.tensor_tensor(ST, ST, pair(4), ALU.add)
                inc(ins)
                after(dve, "dve", st, "s")

        def pool_delta(pool, n):
            quad = lambda b: b.rearrange("p (d h t) -> p d h t", d=2, h=4)
            eight = lambda b: b.rearrange("p (e t) -> p e t", e=8)
            inc = lambda ins: ins.then_inc(s["step_pool"], 1)
            for st in range(6):
                a = step_bc(la, st)
                if st:
                    after(pool, "pe", st - 1, "wt")
                inc(pool.tensor_tensor(quad(LAM_KE), masks(0), a.rearrange("p (d h) t -> p d h t", d=2), ALU.mult))
                if st:
                    after(pool, "pe", st - 1, "y6b")
                inc(pool.tensor_copy(eight(LAB_B), a))
                for l in range(1, 7):
                    if l == 1:
                        after(pool, "dve", st, "nt")
                    elif l == 2:
                        after(pool, "pe", st, "y0")
                    else:
                        after(pool, "pe", st, f"y{l - 2}b")
                    inc(pool.tensor_tensor(quad(DEC_B if l % 2 else LAB_B), quad(NT), masks(4 + 2 * l), ALU.mult))
                after(pool, "act", st, "kt")
                after(pool, "pe", st, "decay")
                inc(pool.tensor_tensor(eight(LAM_KE), eight(KT), step_bc(gates[:, 2], st), ALU.mult))
                after(pool, "pool", st, "ke")
                inc(pool.tensor_tensor(eight(KT), eight(KT), step_bc(kscale, st), ALU.mult))

        def act_silu_gate(act, n, pairs):
            for i, (g, o) in enumerate(pairs):
                act.activation(g, g, ACT.Silu).then_inc(s["gate_ready"], 1)

        def dve_silu_gate(dve, n, pairs):
            for i, (g, o) in enumerate(pairs):
                dve.wait_ge(s["gate_ready"], n.at("gate_ready") + i + 2)
                for a, b in (zip((g[:, 0:CTX], g[:, CTX + 2:GN]), o) if isinstance(o, list) else ((g, o),)):
                    dve.tensor_tensor(b, b, a, ALU.mult)

        bt_a = arena[:, A_BT:A_BT + 105 * 64].rearrange("p (s c) -> p s c", c=64)
        bt_b = sb("bias_tail", [P, 15, 64], F32, "act_hi", (6 * GW + 7) // 8 * 8)

        def pe_bias(pe, n):
            pe.wait_ge(s["rpb_landed"], 16)
            for g in range(16):
                if g >= 8:
                    pe.wait_ge(s["bt_read"], g - 7)
                for q in range(4):
                    c = 4 * g + q
                    mm = pe.matmul(ps[0:64, g % 8, 120 * q:120 * q + 120], band[0:31, 63 - c:127 - c], pa[0:31, 0:120],
                                   start=True, stop=True)
                mm.then_inc(s["bt_ready"], 1)

        def dve_bias(dve, n):
            dve.memset(bt_a[64:128, 0:1, :], 0.0)
            for g in range(16):
                dve.wait_ge(s["bt_ready"], g + 1)
                src = ps[0:64, g % 8, 0:480].rearrange("p (c s) -> p s c", c=4)
                c = slice(4 * g, 4 * g + 4)
                dve.tensor_copy(bt_a[0:64, :, c], src[:, 0:105, :])
                dve.tensor_copy(bt_b[0:64, :, c], src[:, 105:120, :])
                dve.tensor_copy(bt_a[64:128, 1:105, c], src[:, 0:104, :])
                dve.tensor_copy(bt_b[64:128, :, c], src[:, 104:119, :]).then_inc(s["bt_read"], 1)
            dve.wait_ge(s["bt_read"], 16)
            for z, m in ((bt_a, 105), (bt_b, 15)):
                dve.tensor_tensor(z[:, :, :], z[:, :, :], cmask.unsqueeze(1).to_broadcast([P, m, 64]), ALU.add)

        def cut(a, m, w):
            return arena[:, a:a + m * w].rearrange("p (m t) -> p m t", m=m)

        fq = cut(0, 8, T2)
        r3 = cut(8 * T2, 12, T2)
        fv = cut(20 * T2, 5, 512)
        rv = cut(20 * T2 + 2560, 5, 512)
        ncb = cut(20 * T2 + 5120, 8, T2)
        ro = cut(28 * T2 + 5120, 4, T2)
        rflat = sb("ret_bufs", [P, 4 * 512], F32, "act_hi")
        rbuf = [rflat[:, 512 * i:512 * (i + 1)] for i in range(4)]
        HALF = T2 // 2

        cum = ro[0:8, 0, :]
        FTILES = [(META + P * t, P) for t in range(4)] + [(0, META)]

        def pe_forget(pe, n, l):
            b = n.at("forget")
            pe_small_products(pe, n, 8, [(TOK2 + q * HALF, HALF) for q in range(2)]).then_inc(s["f_logits"], 1)
            pe.wait_ge(s["f_cum"], b + 1)
            for t, (c0, rows) in enumerate(FTILES):
                mm = pe.matmul(ps[0:rows, 2, 8 * t:8 * t + 8], cum[:, c0:c0 + rows], ident[0:8, 0:8], start=True, stop=True)
            mm.then_inc(s["f_logits"], 1)
            for e in range(8):
                if e >= 2:
                    pe.wait_ge(s["f_read"], 8 * b + e - 1)
                for q in range(2):
                    mm = pe.matmul(ps[:, 4 + 2 * (e % 2) + q, 0:HALF], ident[0:8, e:e + 1].to_broadcast([8, P]),
                                   cum[:, q * HALF:(q + 1) * HALF], start=True, stop=True)
                mm.then_inc(s["f_rows"], 1)

        def act_forget(act, n, l):
            b = n.at("forget")
            act.wait_ge(s["f_z"], b + 1)
            z, t = ro[0:8, 1, :], ro[0:8, 2, :]
            act_link(act, n, act.activation(t, z, ACT.Abs))
            act_link(act, n, act.activation(t, t, ACT.Exp, scale=-1.0))
            act.activation(t, t, ACT.Ln, bias=1.0).then_inc(s["f_log"], 1)
            for e in range(8):
                act.wait_ge(s["f_rows"], 8 * b + e + 1)
                act.mul(ncb[:, e, :].rearrange("p (a t) -> p a t", a=2), ps[:, 4 + 2 * (e % 2):6 + 2 * (e % 2), 0:HALF], -1.0
                        ).then_inc(s["f_read"], 1)

        def dve_forget(dve, n, l):
            b = n.at("forget")
            z, t = ro[0:8, 1, :], ro[0:8, 2, :]
            dve.memset(ro[0:8, 3, :], 1.0)
            dve.wait_ge(s["f_logits"], 2 * b + 1)
            dve.tensor_scalar(z.rearrange("p (a t) -> p a t", a=2), ps[0:8, 0:2, 0:HALF], vec[0:8, VEC["b_fgate"] + l:VEC["b_fgate"] + l + 1],
                              None, ALU.add).then_inc(s["f_z"], 1)
            dve.wait_ge(s["f_log"], b + 1)
            dve_link(dve, n, dve.scalar_tensor_tensor(z, z, 0.0, t, ALU.min, ALU.subtract))
            dve.tensor_tensor_scan(cum, ro[0:8, 3, :], z, 0.0, ALU.mult, ALU.add).then_inc(s["f_cum"], 1)
            dve.wait_ge(s["f_logits"], 2 * b + 2)
            dve.tensor_copy(small[:, 32:64], ps[:, 2, 0:32])
            dve.tensor_copy(small[0:META, 64:72], ps[0:META, 2, 32:40])

        def act_rotate(act, n, l):
            for i in range(8):
                if i >= 2:
                    act.wait_ge(s["turned"], 8 * l + i - 1)
                act.copy(scr[0:64, i % 2, 0:T2], r3[64:128, i, :])
                act.copy(scr[64:128, i % 2, 0:T2], r3[0:64, i, :]).then_inc(s["swapped"], 1)

        def dve_rotate(dve, n, l):
            for i in range(8):
                k = 1.0 if i < 4 else 128 ** -0.5
                dve_link(dve, n, dve.scalar_tensor_tensor(scr[:, 2 + i % 2, 0:T2], r3[:, i, :], k, pa[:, 0:T2], ALU.mult, ALU.mult))
                dve.wait_ge(s["swapped"], 8 * l + i + 1)
                dve_link(dve, n, dve.scalar_tensor_tensor(scr[:, i % 2, 0:T2], scr[:, i % 2, 0:T2], k, pa[:, T2:2 * T2],
                                                          ALU.mult, ALU.mult))
                dve.tensor_tensor(r3[:, i, :], scr[:, i % 2, 0:T2], scr[:, 2 + i % 2, 0:T2], ALU.add).then_inc(s["turned"], 1)

        CHUNKS = [(0, META, 4)] + [(META + P * c, P, c) for c in range(4)]
        AR, KR, QR, SR = rbuf

        def heads4(buf, rows, cols):
            return buf.rearrange("p (h t) -> p h t", h=4)[0:rows, :, 0:cols]

        def pe_retention(pe, n, l):
            for i, (c0, rows, vt) in enumerate(CHUNKS):
                at = 5 * l + i
                if at:
                    pe.wait_ge(s["r_out"], at)
                for e in range(4):
                    pe.matmul(ps[0:rows, 0, e * P:e * P + rows], r3[:, 4 + e, c0:c0 + rows], r3[:, e, c0:c0 + rows], start=True, stop=True)
                for e in range(4):
                    mm = pe.transpose(ps[0:rows, 1, e * P:e * P + P], r3[:, 4 + e, c0:c0 + rows], ident)
                mm.then_inc(s["r_raw"], 1)
                pe.wait_ge(s["r_scaled"], at + 1)
                for e in range(4):
                    vv = rv[0:rows, vt, e * P:(e + 1) * P]
                    mm = pe.matmul(ps[:, 2, e * P:e * P + rows], vv, heads4(AR, rows, rows)[:, e], start=True, stop=(i == 0))
                    if i:
                        pe.matmul(ps[:, 2, e * P:e * P + rows], heads4(SR, P, P)[:, e], heads4(QR, P, P)[:, e], start=False, stop=True)
                for e in range(4):
                    mm = pe.matmul(ps[:, 3, e * P:(e + 1) * P], heads4(KR, rows, P)[:, e], rv[0:rows, vt, e * P:(e + 1) * P],
                                   start=True, stop=True)
                mm.then_inc(s["r_sums"], 1)

        def dve_retention(dve, n, l):
            dec = ret_tab[:, 0:512].rearrange("p (h t) -> p h t", h=4)
            qd = ret_tab[:, 512:1024].rearrange("p (h t) -> p h t", h=4)
            for i, (c0, rows, vt) in enumerate(CHUNKS):
                at = 5 * l + i
                kd = ret_tab[0:rows, 1024 + (4 if i == 0 else 0):1024 + (8 if i == 0 else 4)]
                dve.wait_ge(s["r_raw"], at + 1)
                if i:
                    dve.tensor_tensor(heads4(QR, P, P), r3[:, 0:4, c0:c0 + P], qd, ALU.mult)
                dve.tensor_tensor(heads4(AR, rows, rows), ps[0:rows, 0, :].rearrange("p (h t) -> p h t", h=4)[:, :, 0:rows],
                                  dec[0:rows, :, 0:rows], ALU.mult)
                dve.tensor_tensor(heads4(KR, rows, P), ps[0:rows, 1, :].rearrange("p (h t) -> p h t", h=4),
                                  kd.unsqueeze(2).to_broadcast([rows, 4, P]), ALU.mult).then_inc(s["r_scaled"], 1)
                dve.wait_ge(s["r_sums"], at + 1)
                dve.tensor_copy(ro[:, :, c0:c0 + rows], ps[:, 2, :].rearrange("p (h t) -> p h t", h=4)[:, :, 0:rows])
                if i:
                    dve_link(dve, n, dve.tensor_tensor(heads4(SR, P, P), heads4(SR, P, P), qd[:, :, P - 1:P].to_broadcast([P, 4, P]),
                                                       ALU.mult))
                    dve_link(dve, n, dve.tensor_tensor(SR, SR, ps[:, 3, :], ALU.add))
                else:
                    dve_link(dve, n, dve.tensor_copy(SR, ps[:, 3, :]))
                dve.tensor_copy(small[:, 30:31], small[:, 29:30]).then_inc(s["r_out"], 1)

        def pe_centre(pe, n, l):
            for e in range(4):
                for q in range(2):
                    mm = pe.matmul(ps[:, 2 * e + q, 0:HALF], ones, ro[:, e, q * HALF:(q + 1) * HALF], start=True, stop=True)
                mm.then_inc(s["means"], 1)

        def dve_centre(dve, n, l):
            for e in range(4):
                dve.wait_ge(s["means"], 4 * l + e + 1)
                y = ro[:, e, :].rearrange("p (a t) -> p a t", a=2)
                dve.scalar_tensor_tensor(y, ps[:, 2 * e:2 * e + 2, 0:HALF], -1.0 / P, y, ALU.mult, ALU.add)

        def pe_final(pe, n):
            for t in range(4):
                for k in range(KD):
                    mm = pe.transpose(ps[:, 2 * t + k // 4, (k % 4) * P:(k % 4 + 1) * P], mix[:, k, CTX + t * P:CTX + (t + 1) * P], ident)
                mm.then_inc(s["final_ready"], 1)

        def dve_final(dve, n):
            for t in range(4):
                dve.wait_ge(s["final_ready"], t + 1)
                dve.tensor_copy(arena[:, t * D:(t + 1) * D], ps[:, 2 * t:2 * t + 2, :].rearrange("p a t -> p (a t)")
                                ).then_inc(s["out_ready"], 1)

        qk = arena[:, 0:8 * T].rearrange("p (m t) -> p m t", m=8)
        v0 = arena[:, A_V:A_V + 6 * 512].rearrange("p (t f) -> p t f", t=6)
        q1 = arena[:, A_Q1:A_Q1 + 8 * LAT].rearrange("p (m t) -> p m t", m=8)
        k1 = arena[:, A_K1:A_K1 + 8 * T].rearrange("p (m t) -> p m t", m=8)
        v1 = arena[:, A_V1:A_V1 + 6 * 1024].rearrange("p (t f) -> p t f", t=6)
        TILES = [(c * P, P) for c in range(NCH)]

        def diff_units():
            units = []
            for e in range(4):
                for t in range(NCH):
                    nk = CTX if t < 2 else T
                    units.append(dict(nq=P, nk=nk, q=[qk[64 * m:64 * m + 64, e, t * P:(t + 1) * P] for m in range(2)],
                                      k=[qk[64 * m:64 * m + 64, 4 + e, :] for m in range(2)],
                                      segs=[(0, 0, nk // 2), (1, nk // 2, nk // 2)], keys=[(c * P, P) for c in range(nk // P)],
                                      v=[v0[:, c, e * P:(e + 1) * P] for c in range(nk // P)], o_part=(0, P),
                                      out=mix[:, e, t * P:(t + 1) * P]))
            return units

        def near_units():
            units = []
            for e in range(8):
                for t in range(4):
                    j0 = 15 * (e % 7) + 7 - 2 * t
                    table = (bt_b if e == 7 else bt_a)[:, j0:j0 + 8, :].rearrange("p s c -> p (s c)")
                    units.append(dict(nq=P, nk=T, q=[q1[:, e, t * P:(t + 1) * P]], k=[k1[:, e, :]],
                                      segs=[(0, 0, CTX), (1, CTX, LAT)], keys=[(c * P, P) for c in range(6)],
                                      bias=[("plain", None), ("table", table)], diag=None,
                                      v=[v1[:, c, e * P:(e + 1) * P] for c in range(6)], o_part=(0, P),
                                      p=len(units) % 2, out=mix[:, e, CTX + t * P:CTX + (t + 1) * P]))
            return units

        def fox_units():
            units = []
            for e in range(8):
                r0 = 64 * (e % 2)
                for t in range(-1, 4):
                    c0, nq = (0, META) if t < 0 else (META + P * t, P)
                    nk = c0 + nq
                    segs = [(0, 0, nk)] if nk <= 512 else [(0, 0, nk // 2), (1, nk // 2, nk // 2)]
                    ct = 32 + 8 * (4 if t < 0 else t) + e
                    arg = ("decay", (small[0:nq, ct:ct + 1], ncb[0:nq, e, :]))
                    units.append(dict(nq=nq, nk=nk, q=[fq[r0:r0 + 64, e // 2, c0:c0 + nq]], k=[fq[r0:r0 + 64, 4 + e // 2, :]],
                                      segs=segs, bias=[arg, arg], diag=c0,
                                      keys=[(META + P * c, P) for c in range(t + 1)] + [(0, META)],
                                      v=[fv[:, c, 64 * e:64 * e + 64] for c in range(t + 1)] + [fv[0:META, 4, 64 * e:64 * e + 64]],
                                      o_part=(r0, 64), p=len(units) % 2,
                                      out=mix[r0:r0 + 64, e // 2, TOK2 + c0:TOK2 + c0 + nq]))
            return units

        ACTS = (act_hi, act_lo, KD)

        def second_tables(eng, n):
            eng.wait_ge(s["meta_landed"], 16)
            eng.wait_ge(s["tables_landed"], 64)

        def walk(eng, n, f):
            def stage(name, counts, *args):
                if name in f:
                    f[name](eng, n, *args)
                for key, k in counts.items():
                    n.add(key, k)

            def ring_turns(turns, **more):
                for key, k in dict(turn=turns, tile_read=2 * turns, block_done=2 * turns, **more).items():
                    n.add(key, k)

            def project(halves, turns, dst, scale=None):
                stage("project", {}, ACTS, halves, turns)
                stage("feed", {}, turns)
                stage("low_parts", {}, turns, FULL)
                stage("copy_out", {}, halves, turns, dst, scale)
                ring_turns(turns)

            def project_tok(tiles, turns, dst):
                stage("project_tok", {}, ACTS, tiles, turns)
                stage("feed", {}, turns)
                stage("low_parts", {}, turns, FULL)
                stage("copy_tok", {}, tiles, turns, dst)
                ring_turns(turns, token_tiles=2 * turns)

            def out_proj(halves, gate):
                n["fresh"] = n.at("parts_ready")
                stage("mix_parts", dict(mix_hi=8, parts_ready=8), halves)
                stage("project", {}, ACTS, halves, 4)
                stage("feed", {}, 4)
                stage("low_parts", {}, 4, FULL)
                stage("residual", {}, halves, 4, gate)
                ring_turns(4)
                end_phase(eng, n)

            def feed_forward(halves, gate):
                for q in range(2):
                    stage("gate_up", {}, halves)
                    stage("gates", {}, halves)
                    stage("low_parts", {}, 11, FULL)
                    stage("gated", {}, halves)
                    ring_turns(11, gate_ready=11, product_step=22)
                    stage("down", {}, halves)
                    stage("feed", {}, 4)
                    stage("low_parts", {}, 4, PART)
                    stage("residual", {}, halves, 4, gate)
                    ring_turns(4)
                end_phase(eng, n)

            def norm(halves, a=None, shift=None, gain=None, last=False):
                stage("norm", dict(squares_ready=8, squares_used=8, roots_ready=1, scaled_ready=0 if last else 8,
                                   modulated=0 if last else 8), halves, a, shift, gain, last)
                if last:
                    end_phase(eng, n)
                else:
                    n["fresh"] = n.at("parts_ready")
                    n.add("parts_ready", KD)

            def head_norm(tiles, matrix, scale, rope=False):
                t = len(tiles)
                stage("head_norm", dict(squares_ready=t, sums_ready=t, roots_ready=t, head_scaled=t), tiles, matrix, scale, rope)
                end_phase(eng, n)

            def attend(units, maps, bias):
                u = len(units)
                stage("attend", dict(scores_ready=u * maps, bias_ready=u * maps, exp_done=u * maps, p_ready=u, pt_psum=u,
                                     pt_copied=u, pv_done=u, o_read=u), units, maps, bias)
                end_phase(eng, n)

            stage("setup", dict(act_chain=0))
            stage("ada", {})
            end_phase(eng, n)
            stage("first_split", {})

            norm(BOTH, 0, 0)
            project(BOTH, 4, lambda m, b: qk[:, m, BOTH[b][0]:BOTH[b][0] + BOTH[b][1]])
            project(BOTH, 8, lambda m, b: gd[:, m, (2, 260)[b]:(2, 260)[b] + BOTH[b][1]])
            project_tok(TILES, 2, v0)
            end_phase(eng, n)
            stage("tables1", {})
            stage("small_split", dict(small_parts=1), 16, 16)
            stage("gates_raw", {})
            end_phase(eng, n)
            head_norm([(qk[:, m, :], qk[:, m, :], v("diff_gain", m // 4), T) for m in range(8)], bo64, 1.0 / 64, rope=True)
            attend(diff_units(), 2, False)
            head_norm([(mix[:, m, :], mix[:, m, :], v("subln"), T) for m in range(4)], ones, 1.0 / P)
            stage("load_masks", {})
            stage("conv", {})
            end_phase(eng, n)
            head_norm([(gd[:, m, 2:2 + GN], gd[:, m, 2:2 + GN], P ** -0.5 if m < 4 else 1.0, GN) for m in range(8)], ones, 1.0)
            stage("gates_tab", {})
            end_phase(eng, n)
            stage("delta", {})
            end_phase(eng, n)
            head_norm([(oacc[:, e, :], mix[:, 4 + e, :], v("gdn_norm"), T) for e in range(4)], ones, 1.0 / P)
            stage("silu_gate", dict(gate_ready=4),
                  [(gd[:, 12 + e, 2:2 + GN], [mix[:, 4 + e, 0:CTX], mix[:, 4 + e, CTX:T]]) for e in range(4)])
            end_phase(eng, n)
            out_proj(BOTH, 16)
            norm(BOTH, 1, 24)
            feed_forward(BOTH, 40)
            stage("load_rpb", {})
            norm(BOTH, 2, 48)
            project(LATENT, 4, lambda m, b: q1[:, m, :])
            project(BOTH, 4, lambda m, b: k1[:, m, BOTH[b][0]:BOTH[b][0] + BOTH[b][1]])
            project_tok(TILES, 4, v1)
            end_phase(eng, n)
            stage("bias", {})
            end_phase(eng, n)
            head_norm([(q1[:, m, :], q1[:, m, :], v("na_gain", 0), LAT) for m in range(8)]
                      + [(k1[:, m, :], k1[:, m, :], v("na_gain", 1), T) for m in range(8)], ones, 1.0 / P)
            attend(near_units(), 1, True)
            stage("load_second", {})
            out_proj(LATENT, 48 + 16)
            norm(LATENT, 3, 48 + 24)
            feed_forward(LATENT, 48 + 40)
            stage("tables2", {})
            for l in range(2):
                norm(SECOND, gain=lambda k, l=l: v("attn_norm", 8 * l + k))
                cols = lambda b: slice(b * HALF, (b + 1) * HALF)
                project(SECOND, 2, lambda m, b: fq[:, m, cols(b)], scale=0.125)
                project(SECOND, 2, lambda m, b: fq[:, 4 + m, cols(b)])
                project(SECOND, 6, lambda m, b: r3[:, m, cols(b)])
                tiles2 = [(TOK2 + c0, rows) for c0, rows in FTILES]
                project_tok(tiles2, 2, fv)
                project_tok(tiles2, 2, rv)
                end_phase(eng, n)
                stage("small_split", dict(small_parts=1), 32 + 16 * l, 8)
                stage("forget", dict(forget=1), l)
                end_phase(eng, n)
                if l == 0:
                    stage("load_forget", {})
                attend(fox_units(), 1, True)
                stage("rotate", {}, l)
                end_phase(eng, n)
                stage("retention", {}, l)
                end_phase(eng, n)
                stage("centre", {}, l)
                end_phase(eng, n)
                head_norm([(ro[:, e, :], mix[:, 4 + e, TOK2:T], v("ret_gn", 4 * l + e), T2) for e in range(4)], ones, 1.0 / P)
                stage("silu_gate", dict(gate_ready=4), [(r3[:, 8 + e, :], mix[:, 4 + e, TOK2:T]) for e in range(4)])
                end_phase(eng, n)
                out_proj(SECOND, None)
                norm(SECOND, gain=lambda k, l=l: v("ffn_norm2", 8 * l + k))
                feed_forward(SECOND, None)
            norm(SECOND, gain=lambda k: v("final", k), last=True)
            stage("final", {})

        @block.tensor
        def _(pe):
            walk(pe, Tally(), dict(
                ada=pe_ada, project=pe_project, project_tok=pe_project_tok, down=pe_down,
                gate_up=pe_gate_up, norm=lambda pe, n, hv, a, sh, g, last: pe_norm(pe, n, hv), head_norm=pe_head_norm, attend=pe_attend,
                gates_raw=pe_gates_raw, gates_tab=pe_gates_tab, delta=pe_delta, bias=pe_bias, forget=pe_forget,
                retention=pe_retention, centre=pe_centre, final=pe_final))

        @block.scalar
        def _(act):
            walk(act, Tally(), dict(small_split=act_small_split,
                setup=act_setup, ada=act_ada, first_split=act_first_split, feed=act_feed, mix_parts=act_mix_parts,
                norm=lambda act, n, hv, a, sh, g, last: act_norm(act, n, hv, a, sh, last), gates=act_gates,
                head_norm=act_head_norm, attend=act_attend, conv=act_conv, gates_tab=act_gates_tab, delta=act_delta,
                silu_gate=act_silu_gate, forget=act_forget, rotate=act_rotate, tables2=second_tables))

        @block.vector
        def _(dve):
            walk(dve, Tally(), dict(small_split=dve_small_split,
                setup=dve_setup, ada=dve_ada, copy_out=dve_copy_out, copy_tok=dve_copy_tok, residual=dve_residual,
                gated=dve_gated, mix_parts=dve_mix_parts, norm=lambda dve, n, hv, a, sh, g, last: dve_norm(dve, n, hv, g, last), head_norm=dve_head_norm,
                attend=dve_attend, conv=dve_conv, gates_raw=dve_gates_raw, gates_tab=dve_gates, delta=dve_delta,
                silu_gate=dve_silu_gate, bias=dve_bias, forget=dve_forget, rotate=dve_rotate, retention=dve_retention,
                centre=dve_centre, final=dve_final, tables2=second_tables, tables1=lambda dve, n: dve.wait_ge(s["tables_landed"], 16)))

        @block.gpsimd
        def _(pool):
            def phase_over(pool, n):
                pool.wait_ge(s["phase_done"], 3 * n.at("phase"))

            def first(pool, n):
                pool.dma_start(pa[:, :], dram["rope1"]).then_inc(s["tables_landed"], 16)
                pool.dma_start(wsmall[:, :, :], dram["gate_w"]).then_inc(s["small_landed"], 16)

            def load_masks(pool, n):
                phase_over(pool, n)
                pool.dma_start(pb_[:, :], dram["masks"]).then_inc(s["tables_landed"], 16)
                pool.wait_ge(s["tables_landed"], 32)

            def load_rpb(pool, n):
                phase_over(pool, n)
                pool.dma_start(pa[0:31, 0:120], dram["rpbT"]).then_inc(s["rpb_landed"], 16)

            def load_second(pool, n):
                phase_over(pool, n)
                pool.dma_start(pa[:, :], dram["rope2"]).then_inc(s["tables_landed"], 16)
                pool.dma_start(ret_tab[:, :], dram["ret"]).then_inc(s["tables_landed"], 16)
                pool.dma_start(wsmall[:, :, 0:8], dram["forget_w0"]).then_inc(s["small_landed"], 16)
                pool.dma_start(x[:, :, TOK2:CTX], dram["metaT"]).then_inc(s["meta_landed"], 16)

            def load_forget(pool, n):
                phase_over(pool, n)
                pool.dma_start(wsmall[:, :, 0:8], dram["forget_w1"]).then_inc(s["small_landed"], 16)

            def delta(pool, n):
                phase_over(pool, n)
                pool_delta(pool, n)

            walk(pool, Tally(free_running=1), dict(setup=first, low_parts=pool_feed, delta=delta, load_masks=load_masks, load_rpb=load_rpb, load_second=load_second,
                                     load_forget=load_forget))


def kernel(**inputs):
    import concourse.bacc as bacc
    from concourse.bass_utils import run_bass_kernel_spmd as run

    a = {k: np.asarray(z) for k, z in inputs.items()}

    def blocks(w):
        k, m = w.shape
        return w.reshape(k // P, P, m // P, P).transpose(2, 1, 0, 3).reshape(m // P, P, k)

    def down(w):
        b = blocks(w).reshape(KD, P, 2, SLOT_K * P)
        return b.transpose(2, 0, 1, 3).reshape(2 * KD, P, SLOT_K * P)

    def gate_up(g, u):
        return np.stack([blocks(g), blocks(u)], 1).reshape(2 * FK, P, D)

    def cols(z):
        return z.reshape(-1, P).T

    def kp(z):
        return z.reshape(-1, P, z.shape[-1]).transpose(1, 0, 2)

    ew, ow = a["even_w_in"][0], a["odd_w_in"][0]
    maps = {
        "xT": kp(a["x"][0].T), "ctxT": kp(a["ctx"][0].T), "metaT": kp(a["meta_tokens_2"].T),
        "ada": np.concatenate([blocks(a["ada_w"][l]) for l in range(2)]).reshape(24, 4, P, D).transpose(0, 2, 1, 3)
        .reshape(24, P, 4 * D),
        "even_in": np.concatenate([blocks(ew[:, 0:1024]), blocks(ew[:, 1536:3072]), blocks(ew[:, 3072:3584]),
                                   blocks(ew[:, 1024:1536])]),
        "gate_w": kp(ew[:, 3584:3600]), "even_out": blocks(a["even_w_out"][0]),
        "odd_in": blocks(ow), "odd_out": blocks(a["odd_w_out"][0]), "rpbT": a["na_rpb"][0].reshape(120, 31).T,
    }
    for l in range(2):
        f = a["ffn_w_in"][l]
        maps[f"gu{l}"] = gate_up(f[:, :FF], f[:, FF:])
        maps[f"dn{l}"] = down(a["ffn_w_out"][l])
        w = a["w_in_2"][l]
        maps[f"in2_{l}"] = np.concatenate([blocks(w[:, lo:lo + 512]) for lo in (0, 512, 1544, 2056, 3080, 1024, 2568)])
        maps[f"forget_w{l}"] = kp(w[:, 1536:1544])
        maps[f"out2_{l}"] = blocks(a["w_out_2"][l])
        maps[f"gu2_{l}"] = gate_up(a["w_gate_2"][l], a["w_up_2"][l])
        maps[f"dn2_{l}"] = down(a["w_down_2"][l])

    def row(z):
        return np.broadcast_to(z.reshape(1, -1), (P, z.size))

    bf = np.zeros((P, 2), np.float32)
    bf[0:8] = a["b_fgate_2"].T
    vecs = {"norm_mix": cols(a["norm_mix"]), "norm_ffn": cols(a["norm_ffn"]), "attn_norm": cols(a["attn_norm_2"]),
            "ffn_norm2": cols(a["ffn_norm_2"]), "final": cols(a["final_norm_2"]),
            "diff_gain": np.concatenate([a["diff_qk_gain"][0].T] * 2, 0), "subln": cols(a["diff_subln"]),
            "gdn_norm": cols(a["gdn_norm"]),
            "conv": a["gdn_conv"][0].T.reshape(12, P, 5).transpose(1, 0, 2).reshape(P, 60),
            "na_gain": a["na_qk_gain"][0].T, "ret_gn": cols(a["ret_gn_2"]), "ada_b": cols(a["ada_b"]), "b_fgate": bf,
            "c": np.stack([cols(a["c"]), cols(a["c_ctx"])], 2).reshape(P, 16),
            "dt_bias": row(a["gdn_dt_bias"]), "a_log": row(a["gdn_a_log"]), "lam": row(a["diff_lambda"])}
    maps["vecs"] = np.concatenate([vecs[k] for k in VEC], 1)
    maps.update(shape_tables())
    maps = {k: np.ascontiguousarray(z) for k, z in maps.items()}

    nc = bacc.Bacc("TRN2", target_bir_lowering=False, num_devices=1)
    dram = {k: nc.dram_tensor(f"in_{k}", z.shape, F32, kind="ExternalInput").ap() for k, z in maps.items()}
    out = nc.dram_tensor("result", (LAT, D), F32, kind="ExternalOutput").ap()
    build(nc, dram, out)
    r = run(nc, [{f"in_{k}": z for k, z in maps.items()}], core_ids=[0])
    return r.results[0]["result"].reshape(1, LAT, D)
```
